# Optimizing a Trainium2 kernel written in Bass

```python
import math
import jax, jax.numpy as jnp
from jax import lax
import numpy as np

D_MODEL = 2048
BATCH = 1
SEQ = 256
DEPTH = 2
DEC_BATCH = 8
DEC_SEQ = 1
PAST_LEN = 1024
PAGE_SIZE = 128

N_A = DEPTH // 2
N_B = DEPTH - N_A
D_RNN = D_MODEL
N_RNN_HEADS = 8
RNN_BLOCK = D_RNN // N_RNN_HEADS
RG_CONV = 4
RG_C = 8.0
N_HEADS = 16
Q_LORA = 512
KV_LORA = 512
NOPE_DIM = 128
ROPE_DIM = 64
V_DIM = 128
ROPE_THETA = 10000.0
ATTN_SCALE = 1.0 / math.sqrt(NOPE_DIM + ROPE_DIM)
Q_BLOCK = 128
D_FF = 3 * D_MODEL
FFN_CONV = 3
EPS = 1e-6

kernel_name = "yoco_rglru_mla_convffn_step"

def rms_norm(x, g):
    xf = x.astype(jnp.float32)
    y = xf * lax.rsqrt(jnp.mean(xf * xf, axis=-1, keepdims=True) + EPS)
    return (y * g.astype(jnp.float32)).astype(x.dtype)

def rope(x, pos):
    half = ROPE_DIM // 2
    inv = ROPE_THETA ** (-jnp.arange(half, dtype=jnp.float32) * 2.0 / ROPE_DIM)
    ang = pos[:, None] * inv[None, :]
    shape = (1, ang.shape[0]) + (1,) * (x.ndim - 3) + (half,)
    cos = jnp.cos(ang).reshape(shape)
    sin = jnp.sin(ang).reshape(shape)
    xf = x.astype(jnp.float32)
    x1, x2 = xf[..., :half], xf[..., half:]
    return jnp.concatenate([x1 * cos - x2 * sin, x2 * cos + x1 * sin], axis=-1).astype(x.dtype)

def causal_dwconv(x, buf, w, b):
    k_w = w.shape[0]
    t = x.shape[1]
    xp = jnp.concatenate([buf.astype(x.dtype), x], axis=1)
    y = b + xp[:, 0:t] * w[0]
    for k in range(1, k_w):
        y = y + xp[:, k:k + t] * w[k]
    return y, xp[:, t:]

def block_diag(x, w):
    xh = x.reshape(x.shape[:-1] + (N_RNN_HEADS, RNN_BLOCK))
    return jnp.einsum('...hi,hij->...hj', xh, w).reshape(x.shape)

def rglru(x, h0, w_a, b_a, w_i, b_i, lam):
    xf = x.astype(jnp.float32)
    r = jax.nn.sigmoid(block_diag(xf, w_a.astype(jnp.float32)) + b_a)
    i = jax.nn.sigmoid(block_diag(xf, w_i.astype(jnp.float32)) + b_i)
    log_a = -RG_C * r * jax.nn.softplus(-lam.astype(jnp.float32))
    a = jnp.exp(log_a)
    u = jnp.sqrt(-jnp.expm1(2.0 * log_a)) * (i * xf)

    def step(h, au):
        a_t, u_t = au
        h = a_t * h + u_t
        return h, h

    h_last, hs = lax.scan(step, h0.astype(jnp.float32), (a.swapaxes(0, 1), u.swapaxes(0, 1)))
    return hs.swapaxes(0, 1).astype(x.dtype), h_last

def recurrent_block(xn, h0, buf0, w_in, conv_w, conv_b, w_a, b_a, w_i, b_i, lam, w_o):
    proj = xn @ w_in
    xb, yb = proj[..., :D_RNN], proj[..., D_RNN:]
    xc, new_buf = causal_dwconv(xb, buf0, conv_w, conv_b)
    hs, h_last = rglru(xc, h0, w_a, b_a, w_i, b_i, lam)
    return (jax.nn.gelu(yb, approximate=True) * hs) @ w_o, h_last, new_buf

def conv_ffn(xn, buf0, w_g, w_u, cw, cb, w_d):
    gc, new_buf = causal_dwconv(xn @ w_g, buf0, cw, cb)
    h = jax.nn.gelu(gc, approximate=True) * (xn @ w_u)
    return h @ w_d, new_buf

def shared_kv(x, pos, kv_in_g, w_dkv, kv_norm_g):
    kv = rms_norm(x, kv_in_g) @ w_dkv
    c = rms_norm(kv[..., :KV_LORA], kv_norm_g)
    kr = rope(kv[..., KV_LORA:], pos)
    return c, kr

def mla_query(xn, pos, w_dq, q_g, w_uq, w_uk):
    cq = rms_norm(xn @ w_dq, q_g)
    q = jnp.einsum('bsl,lhd->bshd', cq, w_uq)
    q_nope, q_rope = q[..., :NOPE_DIM], rope(q[..., NOPE_DIM:], pos)
    q_lat = jnp.einsum('bshd,chd->bshc', q_nope, w_uk)
    return q_lat, q_rope

def prompt_attention(q_lat, q_rope, c, kr):
    b, s, h, cd = q_lat.shape
    nb = s // Q_BLOCK
    qlb = q_lat.reshape(b, nb, Q_BLOCK, h, cd).swapaxes(0, 1)
    qrb = q_rope.reshape(b, nb, Q_BLOCK, h, ROPE_DIM).swapaxes(0, 1)
    k_pos = jnp.arange(s)

    def blk(args):
        ql, qr, bi = args
        sc = (jnp.einsum('bqhc,bkc->bhqk', ql, c).astype(jnp.float32)
              + jnp.einsum('bqhr,bkr->bhqk', qr, kr).astype(jnp.float32)) * ATTN_SCALE
        q_pos = bi * Q_BLOCK + jnp.arange(Q_BLOCK)
        sc = jnp.where(k_pos[None, :] <= q_pos[:, None], sc, -jnp.inf)
        p = jax.nn.softmax(sc, axis=-1).astype(c.dtype)
        return jnp.einsum('bhqk,bkc->bqhc', p, c)

    o = lax.map(blk, (qlb, qrb, jnp.arange(nb)))
    return o.swapaxes(0, 1).reshape(b, s, h, cd)

def sample_attention(q_lat, q_rope, c_new, kr_new, c_past, kr_past):
    t = q_lat.shape[1]
    past = c_past.shape[1]
    s_past = (jnp.einsum('bqhc,bkc->bhqk', q_lat, c_past).astype(jnp.float32)
              + jnp.einsum('bqhr,bkr->bhqk', q_rope, kr_past).astype(jnp.float32)) * ATTN_SCALE
    s_new = (jnp.einsum('bqhc,bkc->bhqk', q_lat, c_new).astype(jnp.float32)
             + jnp.einsum('bqhr,bkr->bhqk', q_rope, kr_new).astype(jnp.float32)) * ATTN_SCALE
    s_new = jnp.where(jnp.tril(jnp.ones((t, t), dtype=bool)), s_new, -jnp.inf)
    p = jax.nn.softmax(jnp.concatenate([s_past, s_new], axis=-1), axis=-1).astype(c_new.dtype)
    return (jnp.einsum('bhqk,bkc->bqhc', p[..., :past], c_past)
            + jnp.einsum('bhqk,bkc->bqhc', p[..., past:], c_new))

def trunk(x, pos, rg_h0, rg_buf0, ffn_buf0, attend, P):
    new_h, new_rg_buf, new_ffn_buf = [], [], []
    c = kr = None
    bsz, t = x.shape[0], x.shape[1]
    for l in range(DEPTH):
        g = P['norm_g'][l]
        xn = rms_norm(x, g[0])
        if l < N_A:
            out, h_last, nb = recurrent_block(
                xn, rg_h0[l], rg_buf0[l], P['w_rg_in'][l], P['conv_rg_w'][l], P['conv_rg_b'][l],
                P['w_rg_a'][l], P['b_rg_a'][l], P['w_rg_i'][l], P['b_rg_i'][l],
                P['rg_lambda'][l], P['w_rg_o'][l])
            new_h.append(h_last)
            new_rg_buf.append(nb)
        else:
            j = l - N_A
            q_lat, q_rope = mla_query(xn, pos, P['w_dq'][j], P['q_norm_g'][j], P['w_uq'][j], P['w_uk'])
            o_lat = attend(q_lat, q_rope, c, kr)
            o = jnp.einsum('bshc,chv->bshv', o_lat, P['w_uv']).reshape(bsz, t, N_HEADS * V_DIM)
            out = o @ P['w_mla_o'][j]
        x = x + rms_norm(out, g[1])
        f, fb = conv_ffn(rms_norm(x, g[2]), ffn_buf0[l], P['w_ffn_g'][l], P['w_ffn_u'][l],
                         P['ffn_conv_w'][l], P['ffn_conv_b'][l], P['w_ffn_d'][l])
        new_ffn_buf.append(fb)
        x = x + rms_norm(f, g[3])
        if l == N_A - 1:
            c, kr = shared_kv(x, pos, P['kv_in_g'], P['w_dkv'], P['kv_norm_g'])
    return x, jnp.stack(new_h), jnp.stack(new_rg_buf), jnp.stack(new_ffn_buf), c, kr

def setup_inputs(seed: int = 0) -> dict:
    key = jax.random.key(seed)
    ks = jax.random.split(key, 40)
    f32 = jnp.float32
    n_pages = PAST_LEN // PAGE_SIZE
    n_phys = (DEC_BATCH * n_pages * 5) // 4

    def nrm(k, shape, fan_in):
        return jax.random.normal(k, shape, f32) * (fan_in ** -0.5)

    a0 = jax.random.uniform(ks[20], (N_A, D_RNN), f32, 0.9, 0.999)
    a_base = a0 ** (1.0 / RG_C)
    rg_lambda = jnp.log(a_base) - jnp.log1p(-a_base)
    page_table = jax.random.permutation(ks[7], n_phys)[:DEC_BATCH * n_pages].reshape(
        DEC_BATCH, n_pages).astype(jnp.int32)
    return {
        'x_prompt': jax.random.normal(ks[0], (BATCH, SEQ, D_MODEL), f32),
        'x_sample': jax.random.normal(ks[1], (DEC_BATCH, DEC_SEQ, D_MODEL), f32),
        'state_rglru_h': 0.5 * jax.random.normal(ks[2], (N_A, DEC_BATCH, D_RNN), f32),
        'state_rglru_conv': jax.random.normal(ks[3], (N_A, DEC_BATCH, RG_CONV - 1, D_RNN), f32),
        'state_ffn_conv': jax.random.normal(ks[4], (DEPTH, DEC_BATCH, FFN_CONV - 1, D_FF), f32),
        'cache_kv_latent': jax.random.normal(ks[5], (n_phys, PAGE_SIZE, KV_LORA), f32),
        'cache_k_rope': jax.random.normal(ks[6], (n_phys, PAGE_SIZE, ROPE_DIM), f32),
        'page_table': page_table,
        'norm_g': 1.0 + 0.05 * jax.random.normal(ks[8], (DEPTH, 4, D_MODEL), f32),
        'w_rg_in': nrm(ks[9], (N_A, D_MODEL, 2 * D_RNN), D_MODEL),
        'conv_rg_w': nrm(ks[10], (N_A, RG_CONV, D_RNN), RG_CONV),
        'conv_rg_b': 0.02 * jax.random.normal(ks[11], (N_A, D_RNN), f32),
        'w_rg_a': nrm(ks[12], (N_A, N_RNN_HEADS, RNN_BLOCK, RNN_BLOCK), RNN_BLOCK),
        'b_rg_a': 0.02 * jax.random.normal(ks[13], (N_A, D_RNN), f32),
        'w_rg_i': nrm(ks[14], (N_A, N_RNN_HEADS, RNN_BLOCK, RNN_BLOCK), RNN_BLOCK),
        'b_rg_i': 0.02 * jax.random.normal(ks[15], (N_A, D_RNN), f32),
        'rg_lambda': rg_lambda,
        'w_rg_o': nrm(ks[16], (N_A, D_RNN, D_MODEL), D_RNN),
        'kv_in_g': 1.0 + 0.05 * jax.random.normal(ks[17], (D_MODEL,), f32),
        'w_dkv': nrm(ks[18], (D_MODEL, KV_LORA + ROPE_DIM), D_MODEL),
        'kv_norm_g': 1.0 + 0.05 * jax.random.normal(ks[19], (KV_LORA,), f32),
        'w_uk': nrm(ks[21], (KV_LORA, N_HEADS, NOPE_DIM), KV_LORA),
        'w_uv': nrm(ks[22], (KV_LORA, N_HEADS, V_DIM), KV_LORA),
        'w_dq': nrm(ks[23], (N_B, D_MODEL, Q_LORA), D_MODEL),
        'q_norm_g': 1.0 + 0.05 * jax.random.normal(ks[24], (N_B, Q_LORA), f32),
        'w_uq': nrm(ks[25], (N_B, Q_LORA, N_HEADS, NOPE_DIM + ROPE_DIM), Q_LORA),
        'w_mla_o': nrm(ks[26], (N_B, N_HEADS * V_DIM, D_MODEL), N_HEADS * V_DIM),
        'w_ffn_g': nrm(ks[27], (DEPTH, D_MODEL, D_FF), D_MODEL),
        'w_ffn_u': nrm(ks[28], (DEPTH, D_MODEL, D_FF), D_MODEL),
        'ffn_conv_w': nrm(ks[29], (DEPTH, FFN_CONV, D_FF), FFN_CONV),
        'ffn_conv_b': 0.02 * jax.random.normal(ks[30], (DEPTH, D_FF), f32),
        'w_ffn_d': nrm(ks[31], (DEPTH, D_FF, D_MODEL), D_FF),
    }

def reference(x_prompt, x_sample, state_rglru_h, state_rglru_conv, state_ffn_conv,
              cache_kv_latent, cache_k_rope, page_table, norm_g, w_rg_in, conv_rg_w,
              conv_rg_b, w_rg_a, b_rg_a, w_rg_i, b_rg_i, rg_lambda, w_rg_o, kv_in_g, w_dkv,
              kv_norm_g, w_uk, w_uv, w_dq, q_norm_g, w_uq, w_mla_o, w_ffn_g, w_ffn_u,
              ffn_conv_w, ffn_conv_b, w_ffn_d):
    P = {'norm_g': norm_g, 'w_rg_in': w_rg_in, 'conv_rg_w': conv_rg_w, 'conv_rg_b': conv_rg_b,
         'w_rg_a': w_rg_a, 'b_rg_a': b_rg_a, 'w_rg_i': w_rg_i, 'b_rg_i': b_rg_i,
         'rg_lambda': rg_lambda, 'w_rg_o': w_rg_o, 'kv_in_g': kv_in_g, 'w_dkv': w_dkv,
         'kv_norm_g': kv_norm_g, 'w_uk': w_uk, 'w_uv': w_uv, 'w_dq': w_dq,
         'q_norm_g': q_norm_g, 'w_uq': w_uq, 'w_mla_o': w_mla_o, 'w_ffn_g': w_ffn_g,
         'w_ffn_u': w_ffn_u, 'ffn_conv_w': ffn_conv_w, 'ffn_conv_b': ffn_conv_b,
         'w_ffn_d': w_ffn_d}
    bsz, s = x_prompt.shape[0], x_prompt.shape[1]
    dbsz, t = x_sample.shape[0], x_sample.shape[1]

    pos_p = jnp.arange(s, dtype=jnp.float32)
    h0_p = jnp.zeros((N_A, bsz, D_RNN), jnp.float32)
    rgb0_p = jnp.zeros((N_A, bsz, RG_CONV - 1, D_RNN), x_prompt.dtype)
    ffb0_p = jnp.zeros((DEPTH, bsz, FFN_CONV - 1, D_FF), x_prompt.dtype)
    y_prompt, p_rglru_h, p_rglru_conv, p_ffn_conv, p_kv_latent, p_k_rope = trunk(
        x_prompt, pos_p, h0_p, rgb0_p, ffb0_p, prompt_attention, P)

    c_past = cache_kv_latent[page_table].reshape(dbsz, -1, KV_LORA)
    kr_past = cache_k_rope[page_table].reshape(dbsz, -1, ROPE_DIM)
    past_len = c_past.shape[1]
    pos_s = past_len + jnp.arange(t, dtype=jnp.float32)

    def attend_sample(q_lat, q_rope, c_new, kr_new):
        return sample_attention(q_lat, q_rope, c_new, kr_new, c_past, kr_past)

    y_sample, s_rglru_h, s_rglru_conv, s_ffn_conv, s_kv_latent, s_k_rope = trunk(
        x_sample, pos_s, state_rglru_h, state_rglru_conv, state_ffn_conv, attend_sample, P)

    return (y_prompt, y_sample, p_rglru_h, s_rglru_h, p_rglru_conv, s_rglru_conv,
            p_ffn_conv, s_ffn_conv, p_kv_latent, s_kv_latent, p_k_rope, s_k_rope)


_drawn_inputs = setup_inputs


def setup_inputs(seed=0):
    import zlib

    import numpy as np

    out = dict(_drawn_inputs(seed))
    spreads = {}
    factors = {'b_rg_a': 8.0, 'b_rg_i': 6.91, 'ffn_conv_b': 3.412}
    for name, (base, spread) in spreads.items():
        noise = np.random.default_rng([zlib.crc32(name.encode()), seed]).standard_normal(out[name].shape)
        drawn = base * np.exp(spread * noise) if base else spread * noise
        out[name] = __import__('jax').numpy.asarray(drawn.astype(out[name].dtype))
    for name, factor in factors.items():
        out[name] = (out[name] * factor).astype(out[name].dtype)
    return out
```

```python
from contextlib import ExitStack

import concourse.bass as bass
from concourse import mybir

F32 = mybir.dt.float32
F32R = mybir.dt.float32r
I32 = mybir.dt.int32
ALU = mybir.AluOpType
ACT = mybir.ActivationFunctionType
AX = mybir.AxisListType
ds = bass.ds

P = 128
D = 2048
KT = D // P
S = 256
NB = 8
T = S + NB
FF = 3 * D
FT = FF // P
SECTIONS = FF // D
H = 16
NOPE, ROPE, LORA = 128, 64, 512
LT = LORA // P
PAGES, PAGE = 8, 128
PHYS = (NB * PAGES * 5) // 4
KEYS = PAGES * PAGE + NB
ATTN_SCALE = 1.0 / float(NOPE + ROPE) ** 0.5
EPS = 1e-6
RG_C = 8.0
LG = 8

RAW, SPLIT = 8, 4
FFN_CHUNKS = SECTIONS * (64 + 32)
FFN_PAIRS = SECTIONS * (16 + 8)
C_RGX = 0
C_RGY = C_RGX + 32
C_RGO = C_RGY + 32
C_FFN0 = C_RGO + 32
C_DKV = C_FFN0 + FFN_CHUNKS
C_DQ = C_DKV + 12
C_UQ = C_DQ + 8
C_UK = C_UQ + 12
C_UV = C_UK + 8
C_MO = C_UV + 8
C_FFN1 = C_MO + 32
C_END = C_FFN1 + FFN_CHUNKS
G_RGX = 0
G_RGY = G_RGX + 8
G_RGO = G_RGY + 8
G_FFN0 = G_RGO + 8
G_DKV = G_FFN0 + FFN_PAIRS
G_DQ = G_DKV + 3
G_UQ = G_DQ + 2
G_UK = G_UQ + 12
G_UV = G_UK + 8
G_MO = G_UV + 8
G_FFN1 = G_MO + 8
G_END = G_FFN1 + FFN_PAIRS

RG_ROWS = 3 * NB + 4 + 1
GATE_ROWS = 3 + NB
FF_ROWS = 2 * NB + 3 + 1
PT_RG = 0
PT_GATE = PT_RG + RG_ROWS * KT
PT_FF = PT_GATE + GATE_ROWS * KT
PT_NORM = PT_FF + 2 * FF_ROWS * FT
PT_KVIN = PT_NORM + 8 * KT
PT_KVN = PT_KVIN + KT
PT_QN = PT_KVN + LT
PT_END = PT_QN + LT
PT_TILES = -(-PT_END // P)

K_ID = 0
K_COS = K_ID + P
K_SIN = K_COS + T
K_MASK = K_SIN + T
K_OWN = K_MASK + P
K_SWAP = K_OWN + NB * NB
K_END = K_SWAP + P

CS_FFN0 = 7 * KT
CS_FFN1 = CS_FFN0 + 5 * FT
H_FFN0 = KT
H_FFN1 = H_FFN0 + FT
XN_0, XN_1, XN_KV, XN_Q, XN_3 = (KT * n for n in range(5))
PAR_STEPS = 19

N_X0, N_RGO, N_X1, N_F0, N_X2, N_C, N_CQ, N_MO, N_X3, N_F1 = range(10)


def parts(c):
    if C_DKV + 8 <= c < C_DQ:
        return 2
    if C_UQ <= c < C_UK:
        return 4 if (c - C_UQ) % 3 == 2 else 2
    return 1


def parts_before(c):
    return sum(parts(d) - 1 for d in range(C_DKV, min(c + 1, C_UK)) if d % RAW == c % RAW)


def loaded(c):
    return 16 * (c // RAW + 1 + parts_before(c))


class Semaphores:
    pass


def build(nc, I, O):
    with ExitStack() as ctx:
        def sem(name):
            return ctx.enter_context(nc.semaphore(name))

        at = [16512]

        def sb(name, shape, dt, offset=None):
            size = 4
            for n in shape[1:]:
                size *= n
            if offset is None:
                offset = at[0]
                at[0] += -(-size // 32) * 32
            assert offset + size <= 229344, (name, offset + size)
            return nc.alloc_sbuf_tensor_at(name, list(shape), dt, offset=offset)

        x = sb("x", [P, KT, T], F32)
        raw = sb("raw", [P, RAW, 4, 256], F32)
        hi = sb("hi", [P, SPLIT, 4, 256], F32R)
        lo = sb("lo", [P, SPLIT, 4, 256], F32R)
        pt_at = at[0]
        PT = sb("PT", [P, PT_END], F32)
        kc = sb("kc", [P, K_END], F32)
        ones = sb("ones", [P, P], F32)
        rx = sb("rx", [P, T], F32)
        rf = sb("rf", [P, T], F32)
        ssum = sb("ssum", [P, T], F32)
        mean = sb("mean", [P, T], F32)
        rg_tail = sb("rg_tail", [P, KT, 3 + NB], F32)
        h_tail = sb("h_tail", [P, KT, 1 + NB], F32)
        ptab = sb("ptab", [1, NB * PAGES], I32)
        ff_at = at[0]
        ff_tail = sb("ff_tail", [P, FT, 2 + NB], F32)
        xn_at = at[0]
        xnh = sb("xnh", [P, KT, T], F32R)
        xnl_at = at[0]
        xnl = sb("xnl", [P, KT, T], F32R)
        h_at = at[0]
        hh = sb("hh", [P, KT, T], F32R)
        hl = sb("hl", [P, KT, T], F32R)
        f_at = at[0]
        f = sb("f", [P, KT, T], F32)
        free_at = at[0]
        TILE2 = 2 * T * 4
        ptrows = sb("ptrows", [P, PT_TILES, P], F32, xn_at)
        xrows = sb("xrows", [P, 2, D], F32, f_at)
        xsrows = sb("xsrows", [NB, D], F32, free_at)
        soft = sb("soft", [P, 4, KT], F32, free_at + D * 4)
        sq_xn = sb("sq_xn", [P, KT, T], F32, xn_at)
        sq_h = sb("sq_h", [P, KT, T], F32, h_at)
        gs = sb("gs", [P, 2, T], F32, free_at)
        ge = sb("ge", [P, 2, T], F32, free_at + TILE2)
        cv = sb("cv", [P, 2, T], F32, free_at + 2 * TILE2)
        us = sb("us", [P, 2, T], F32, free_at + 3 * TILE2)
        cwf = sb("cwf", [P, FF_ROWS, 2], F32, free_at + 4 * TILE2)
        ta = sb("ta", [P, 2, T], F32, free_at + 2 * TILE2)
        ti = sb("ti", [P, 2, T], F32, free_at + 3 * TILE2)
        r1 = sb("r1", [P, 2, T], F32, free_at + 4 * TILE2)
        aa = sb("aa", [P, 2, T], F32, free_at + 5 * TILE2)
        sq = sb("sq", [P, 2, T], F32, free_at + 6 * TILE2)
        gw_at = free_at + 7 * TILE2
        gw = sb("gw", [P, 2, 4, 256], F32, gw_at)
        cwr = sb("cwr", [P, RG_ROWS, 2], F32, ff_at)
        gp = sb("gp", [P, GATE_ROWS, 2], F32, ff_at + 256)
        cT = sb("cT", [P, LT, T], F32, free_at)
        cTh = sb("cTh", [P, LT, T], F32R, free_at + 2 * TILE2)
        cTl = sb("cTl", [P, LT, T], F32R, free_at + 4 * TILE2)
        krT = sb("krT", [P, T], F32, free_at + 6 * TILE2)
        mla_at = free_at + 6 * TILE2 + T * 4
        cqh = sb("cqh", [P, LT, T], F32R, mla_at)
        cql = sb("cql", [P, LT, T], F32R, mla_at + 2 * TILE2)
        pre = sb("pre", [P, LT, T], F32, f_at)
        prk = sb("prk", [P, T], F32, f_at + 2 * TILE2)
        sqs = sb("sqs", [P, LT, T], F32, f_at + 3 * TILE2)
        preq = sb("preq", [P, LT, T], F32, f_at + 5 * TILE2)
        rot = sb("rot", [P, 2, T], F32, f_at + 7 * TILE2)
        qn = sb("qn", [P, H, T], F32, xn_at)
        qr = sb("qr", [P, H // 2, T], F32, xnl_at)
        mid_at = xnl_at + 4 * TILE2
        ukT = sb("ukT", [P, 2, LORA], F32, h_at)
        qlat = sb("qlat", [P, LT, NB, H], F32, mid_at)
        olat = sb("olat", [P, LT, H, NB], F32, mid_at + 2048)
        cnew = sb("cnew", [NB, LORA], F32, mid_at + 4096)
        qrs = sb("qrs", [ROPE, NB, H], F32, mid_at + 6144)
        qb = sb("qb", [P, LT, H], F32, mid_at + 6656)
        qrb = sb("qrb", [ROPE, H], F32, mid_at + 6912)
        stats = sb("stats", [P, 16], F32, mid_at + 6976)
        kn = sb("kn", [P, H, S], F32, f_at)
        cpage = sb("cpage", [P, 4, 4, LORA], F32, h_at)
        kpage = sb("kpage", [P, 4, 4, ROPE], F32, mla_at)
        ctp = sb("ctp", [P, 2, LT, P], F32, mla_at + 4096)
        krp = sb("krp", [ROPE, 2, P], F32, mla_at + 8192)
        sp_ = sb("sp_", [H, KEYS], F32, pt_at)
        spT = sb("spT", [P, PAGES + 1, H], F32, pt_at + KEYS * 4)
        Vs = sb("Vs", [P, 2, 2, 256], F32, mla_at)
        sm = sb("sm", [P, 2, 3 * P], F32, mla_at + 4096)
        pTs = sb("pTs", [P, 3 * P], F32, mla_at + 7168)
        rows = sb("rows", [P, 2, 512], F32, h_at + 2 * P * 4 * 16)
        yrows = sb("yrows", [P, 2, 512], F32, h_at)

        acc = [ctx.enter_context(nc.psum_tensor(f"acc{n}", [P, 512], F32)) for n in range(4)]
        mis = [ctx.enter_context(nc.psum_tensor(f"mis{n}", [P, 512], F32)) for n in range(4)]

        ident = kc[:, K_ID:K_ID + P]
        cos_ = kc[:, K_COS:K_COS + T]
        sin_ = kc[:, K_SIN:K_SIN + T]
        mask = kc[:, K_MASK:K_MASK + P]
        swap = kc[:, K_SWAP:K_SWAP + P]

        def gain(l, n, j):
            c = PT_NORM + (l * 4 + n) * KT + j
            return PT[:, c:c + 1]

        def pcol(base, j):
            return PT[:, base + j:base + j + 1]

        s = Semaphores()
        s.hi_ready = sem("hi_ready")
        s.lo_ready = sem("lo_ready")
        s.chunk_used = sem("chunk_used")
        s.acc_read = sem("acc_read")
        s.const_in = sem("const_in")
        s.rows_in = sem("rows_in")
        s.x_in = sem("x_in")
        s.ones_set = sem("ones_set")
        s.turned = sem("turned")
        s.pt_ready = sem("pt_ready")
        s.x_turned = sem("x_turned")
        s.par_step = sem("par_step")
        s.sq_done = sem("sq_done")
        s.sum_ready = sem("sum_ready")
        s.stat_ready = sem("stat_ready")
        s.mean_step = sem("mean_step")
        s.rstd_ready = sem("rstd_ready")
        s.fnorm = sem("fnorm")
        s.x_tile = sem("x_tile")
        s.xn_hi = sem("xn_hi")
        s.xn_ready = sem("xn_ready")
        s.cw_ready = sem("cw_ready")
        s.conv_step = sem("conv_step")
        s.tail_saved = sem("tail_saved")
        s.gelu_done = sem("gelu_done")
        s.h_full = sem("h_full")
        s.h_hi = sem("h_hi")
        s.h_ready = sem("h_ready")
        s.gates = sem("gates")
        s.gate_par = sem("gate_par")
        s.gate_tanh = sem("gate_tanh")
        s.gate_th = sem("gate_th")
        s.gate_step = sem("gate_step")
        s.ht_saved = sem("ht_saved")
        s.f_zero = sem("f_zero")
        s.c_step = sem("c_step")
        s.c_hi = sem("c_hi")
        s.c_ready = sem("c_ready")
        s.kr_rot = sem("kr_rot")
        s.kr_step = sem("kr_step")
        s.q_rot = sem("q_rot")
        s.q_step = sem("q_step")
        s.uk_turned = sem("uk_turned")
        s.uk_read = sem("uk_read")
        s.ql_done = sem("ql_done")
        s.ql_ready = sem("ql_ready")
        s.sh_done = sem("sh_done")
        s.sh_ready = sem("sh_ready")
        s.cn_turned = sem("cn_turned")
        s.cn_ready = sem("cn_ready")
        s.ptab_in = sem("ptab_in")
        s.pg_turned = sem("pg_turned")
        s.pg_c = sem("pg_c")
        s.pg_k = sem("pg_k")
        s.pg_scored = sem("pg_scored")
        s.qb_ready = sem("qb_ready")
        s.s_scored = sem("s_scored")
        s.s_step = sem("s_step")
        s.s_exp = sem("s_exp")
        s.s_prob = sem("s_prob")
        s.s_turned = sem("s_turned")
        s.s_pT = sem("s_pT")
        s.s_out = sem("s_out")
        s.ol_ready = sem("ol_ready")
        s.scored = sem("scored")
        s.sm_step = sem("sm_step")
        s.sm_exp = sem("sm_exp")
        s.prob = sem("prob")
        s.p_turned = sem("p_turned")
        s.pT_ready = sem("pT_ready")
        s.o_ps = sem("o_ps")
        s.o_hi = sem("o_hi")
        s.o_ready = sem("o_ready")
        s.out_turned = sem("out_turned")
        s.out_rows = sem("out_rows")
        s.shifted = sem("shifted")
        s.raw_loaded = [sem(f"raw_loaded{n}") for n in range(RAW)]
        s.gw_loaded = [sem(f"gw_loaded{n}") for n in range(2)]
        s.page_in = [sem(f"page_in{n}") for n in range(4)]
        s.out_sent = [sem(f"out_sent{n}") for n in range(2)]
        block = ctx.enter_context(nc.Block())

        def out_plan_mid():
            for g in range(KT // 4):
                yield [rg_tail[:, 4 * g + k, :] for k in range(4)], 3 + NB, [
                    (O["p_rgc"][0, 0, :, 512 * g:512 * g + 512], 0, 3),
                    (O["s_rgc"][0, :, 2, 512 * g:512 * g + 512], 3, NB)]
            for g in range(KT // 4):
                yield [h_tail[:, 4 * g + k, :] for k in range(4)], 1 + NB, [
                    (O["p_h"][0, :, 512 * g:512 * g + 512], 0, 1),
                    (O["s_h"][0, :, 512 * g:512 * g + 512], 1, NB)]
            yield from out_plan_ff(0)

        def out_plan_ff(l):
            for g in range(FT // 4):
                yield [ff_tail[:, 4 * g + k, :] for k in range(4)], 2 + NB, [
                    (O["p_ffc"][l, 0, :, 512 * g:512 * g + 512], 0, 2),
                    (O["s_ffc"][l, :, 1, 512 * g:512 * g + 512], 2, NB)]

        def out_plan_c():
            for t in range(2):
                yield [cT[:, k, t * P:(t + 1) * P] for k in range(LT)], P, [
                    (O["p_kv"][0, t * P:(t + 1) * P, :], 0, P)]
            yield [cT[:, k, S:T] for k in range(LT)], NB, [(O["s_kv"][:, 0, :], 0, NB)]
            for t in range(2):
                yield [krT[0:ROPE, t * P:(t + 1) * P]], P, [(O["p_kr"][0, t * P:(t + 1) * P, :], 0, P)]
            yield [krT[0:ROPE, S:T]], NB, [(O["s_kr"][:, 0, :], 0, NB)]

        def out_plan_y():
            for g in range(KT // 4):
                for t in range(2):
                    yield [x[:, 4 * g + k, t * P:(t + 1) * P] for k in range(4)], P, [
                        (O["y_p"][0, t * P:(t + 1) * P, 512 * g:512 * g + 512], 0, P)]
                yield [x[:, 4 * g + k, S:T] for k in range(4)], NB, [
                    (O["y_s"][:, 0, 512 * g:512 * g + 512], 0, NB)]

        mid = list(out_plan_mid()) + list(out_plan_c())
        end = list(out_plan_ff(1)) + list(out_plan_y())
        plan = mid + end
        out_sems = []
        sent = [0, 0]
        for n, (_, _, dst) in enumerate(plan):
            sent[n % 2] += 16 * len(dst)
            out_sems.append(sent[n % 2])

        def row_slot(n):
            return (rows if n < len(mid) else yrows)[:, n % 2, :]

        def row_width(tiles):
            return sum(t.shape[0] for t in tiles)

        @block.sync
        def _(sp):
            def chunk(c, src, dst=None, off=0, part=0):
                if part == 0 and c >= RAW:
                    sp.wait_ge(s.lo_ready, off + (c - RAW + 1))
                if part == 0 and C_UK <= c - RAW < C_UV:
                    sp.wait_ge(s.chunk_used, off + (c - RAW + 1))
                if part == 0 and C_UV <= c - RAW < C_MO:
                    sp.wait_ge(s.o_ps, off + 2 * (c - RAW - C_UV + 1))
                dst = raw[:, c % RAW, :, :] if dst is None else dst
                sp.dma_start(dst, src).then_inc(s.raw_loaded[c % RAW], 16)

            def rows4(w, q, col, n=256):
                return w[512 * q:512 * q + 512, ds(col, n)].rearrange("(k p) n -> p k n", p=P)

            def stream(w, c0, col0, pairs):
                with sp.Fori(0, pairs // 2) as i:
                    for a in range(2):
                        for q in range(4):
                            chunk(c0 + 4 * a + q, rows4(w, q, i * 512 + (col0 + 256 * a)), off=i * 8)

            def ffn(l, c0):
                with sp.Fori(0, SECTIONS) as sec:
                    with sp.Fori(0, 8) as i:
                        for a, w in enumerate((I["w_ffn_g"], I["w_ffn_u"])):
                            for q in range(4):
                                chunk(c0 + 4 * a + q, rows4(w[l], q, sec * D + i * 256),
                                      off=sec * 96 + i * 8)
                    with sp.Fori(0, 4) as i:
                        for a in range(2):
                            for q in range(4):
                                w = I["w_ffn_d"][l][ds(sec * D + 512 * q, 512), ds(i * 512 + 256 * a, 256)]
                                chunk(c0 + 64 + 4 * a + q, w.rearrange("(k p) n -> p k n", p=P),
                                      off=sec * 96 + i * 8)

            for a in range(2):
                for q in range(4):
                    chunk(C_RGX + 4 * a + q, rows4(I["w_rg_in"][0], q, 256 * a))
            stream(I["w_rg_in"][0], C_RGX + 8, 512, 6)
            stream(I["w_rg_in"][0], C_RGY, D, 8)
            stream(I["w_rg_o"][0], C_RGO, 0, 8)
            ffn(0, C_FFN0)
            for a in range(2):
                for q in range(4):
                    chunk(C_DKV + 4 * a + q, rows4(I["w_dkv"], q, 256 * a))
            for q in range(4):
                for e in range(2):
                    c = C_DKV + 8 + q
                    chunk(c, rows4(I["w_dkv"], q, LORA, ROPE),
                          raw[:, c % RAW, :, ROPE * e:ROPE * e + ROPE], part=e)
            for a in range(2):
                for q in range(4):
                    chunk(C_DQ + 4 * a + q, rows4(I["w_dq"][0], q, 256 * a))
            for g in range(4):
                for e in range(3):
                    c = C_UQ + 3 * g + e
                    for m in range(parts(c)):
                        if e < 2:
                            src = I["w_uq"][0, :, 4 * g + 2 * e + m, 0:NOPE]
                            dst = raw[:, c % RAW, :, NOPE * m:NOPE * (m + 1)]
                        else:
                            src = I["w_uq"][0, :, 4 * g + m, NOPE:NOPE + ROPE]
                            dst = raw[:, c % RAW, :, ROPE * m:ROPE * (m + 1)]
                        chunk(c, src.rearrange("(k p) n -> p k n", p=P), dst, part=m)
            for u in range(8):
                chunk(C_UK + u, rows4(I["w_uk"].rearrange("c h d -> c (h d)"), 0, 256 * u))
            for u in range(8):
                chunk(C_UV + u, rows4(I["w_uv"].rearrange("c h d -> c (h d)"), 0, 256 * u))
            sp.wait_ge(s.ptab_in, 16)
            sp.wait_ge(s.ql_done, H)
            sp.wait_ge(s.out_sent[0], out_sems[len(mid) - 1 - (len(mid) - 1) % 2])
            sp.wait_ge(s.out_sent[1], out_sems[len(mid) - 1 - len(mid) % 2])
            kcache = I["cache_k_rope"]
            ccache = I["cache_kv_latent"]

            def half(i, n, first):
                if not first:
                    sp.wait_ge(s.s_out, i * 2 + (n // 2 - 1))
                for g in range(4):
                    page = sp.value_load(ptab[0:1, ds(i * 16 + (4 * n + g), 1)], min_val=0, max_val=PHYS - 1)
                    sp.dma_start(cpage[:, n, g, :], ccache[ds(page, 1), :, :].rearrange("a k c -> k (a c)"))\
                        .then_inc(s.page_in[n], 16)
                    sp.dma_start(kpage[:, n, g, :], kcache[ds(page, 1), :, :].rearrange("a k c -> k (a c)"))\
                        .then_inc(s.page_in[n], 16)

            for n in range(4):
                half(0, n, True)
            with sp.Fori(1, NB // 2) as i:
                for n in range(4):
                    half(i, n, False)
            for a in range(2):
                for q in range(4):
                    chunk(C_MO + 4 * a + q, rows4(I["w_mla_o"][0], q, 256 * a))
            stream(I["w_mla_o"][0], C_MO + 8, 512, 6)
            ffn(1, C_FFN1)

        row_plan = []
        row_plan += [
            (PT_RG, I["state_rglru_conv"].rearrange("a b k (j p) -> (a b k j) p", p=P)),
            (PT_RG + 3 * NB * KT, I["conv_rg_w"].rearrange("a k (j p) -> (a k j) p", p=P)),
            (PT_RG + (3 * NB + 4) * KT, I["conv_rg_b"].rearrange("a (j p) -> (a j) p", p=P)),
            (PT_GATE, I["b_rg_a"].rearrange("a (j p) -> (a j) p", p=P)),
            (PT_GATE + KT, I["b_rg_i"].rearrange("a (j p) -> (a j) p", p=P)),
            (PT_GATE + 2 * KT, I["rg_lambda"].rearrange("a (j p) -> (a j) p", p=P)),
            (PT_GATE + 3 * KT, I["state_rglru_h"].rearrange("a b (j p) -> (a b j) p", p=P)),
            (PT_NORM, I["norm_g"].rearrange("l n (j p) -> (l n j) p", p=P)),
            (PT_KVIN, I["kv_in_g"].rearrange("(j p) -> j p", p=P)),
            (PT_KVN, I["kv_norm_g"].rearrange("(j p) -> j p", p=P)),
            (PT_QN, I["q_norm_g"].rearrange("a (j p) -> (a j) p", p=P)),
        ]
        for l in range(2):
            base = PT_FF + l * FF_ROWS * FT
            row_plan += [
                (base, I["state_ffn_conv"][l].rearrange("b k (j p) -> (b k j) p", p=P)),
                (base + 2 * NB * FT, I["ffn_conv_w"][l].rearrange("k (j p) -> (k j) p", p=P)),
                (base + (2 * NB + 3) * FT, I["ffn_conv_b"][l:l + 1].rearrange("a (j p) -> (a j) p", p=P)),
            ]
        row_pieces = []
        for base, src in row_plan:
            r = 0
            while r < src.shape[0]:
                t, q = divmod(base + r, P)
                m = min(src.shape[0] - r, P - q)
                row_pieces.append((q, t, src[r:r + m, :]))
                r += m

        @block.gpsimd
        def _(pool):
            pool.dma_start(kc[:, :], I["consts"]).then_inc(s.const_in, 16)
            for q, t, src in row_pieces:
                pool.dma_start(ptrows[q:q + src.shape[0], t, :], src).then_inc(s.rows_in, 16)
            pool.dma_start(ptab[0:1, :], I["page_table"].rearrange("(a b) n -> a (b n)", a=1)).then_inc(s.ptab_in, 16)
            pool.dma_start(O["s_rgc"][0, :, 0:2, :], I["state_rglru_conv"][0, :, 1:3, :]).then_inc(s.shifted, 16)
            pool.dma_start(O["s_ffc"][:, :, 0, :].rearrange("l b f -> (l b) f"),
                           I["state_ffn_conv"][:, :, 1, :].rearrange("l b f -> (l b) f")).then_inc(s.shifted, 16)

            def columns(dst, base, nrows, tiles, first):
                src = PT[:, base:base + nrows * tiles].rearrange("p (r j) -> p r j", j=tiles)
                return pool.tensor_copy(dst, src[:, :, ds(first, 2)])

            pool.wait_ge(s.pt_ready, 6)
            with pool.Fori(0, 8) as i:
                pool.wait_ge(s.conv_step, i * 14)
                columns(cwr[:, :, :], PT_RG, RG_ROWS, KT, i * 2).then_inc(s.cw_ready, 1)
                pool.wait_ge(s.acc_read, i * 2 + 2)
                pool.tensor_copy(rg_tail[:, ds(i * 2, 2), :], gs[:, :, S - 3:T]).then_inc(s.tail_saved, 1)
            pool.wait_ge(s.par_step, PAR_STEPS)
            with pool.Fori(0, 4) as i:
                for a in range(2):
                    pool.wait_ge(s.gates, i * 2 + (a if a == 0 else 0))
                    for e, w in enumerate((I["w_rg_a"], I["w_rg_i"])):
                        src = w[0, ds(i * 2 + a, 1), :, :].rearrange("h (k p) n -> p (h k) n", p=P)
                        pool.dma_start(gw[:, a, 2 * e:2 * e + 2, :], src).then_inc(s.gw_loaded[a], 16)
                for a in range(2):
                    pool.wait_ge(s.gate_step, i * 20 + 10 * a)
                    columns(gp[:, :, :], PT_GATE, GATE_ROWS, KT, i * 4 + 2 * a).then_inc(s.gate_par, 1)
                    pool.wait_ge(s.gate_step, i * 20 + 10 * a + 10)
                    pool.tensor_copy(h_tail[:, ds(i * 4 + 2 * a, 2), :],
                                     f[:, ds(i * 4 + 2 * a, 2), S - 1:T]).then_inc(s.ht_saved, 1)

            def ffn(l, cs0, cw0, xt):
                pool.wait_ge(s.x_tile, xt)
                pool.memset(f[:, :, :], 0.0).then_inc(s.f_zero, 1)
                with pool.Fori(0, SECTIONS) as sec:
                    with pool.Fori(0, 8) as i:
                        pool.wait_ge(s.conv_step, sec * 80 + i * 10 + cs0)
                        columns(cwf[:, :, :], PT_FF + l * FF_ROWS * FT, FF_ROWS, FT, sec * 16 + i * 2)\
                            .then_inc(s.cw_ready, 1)
                        g = G_FFN0 if l == 0 else G_FFN1
                        pool.wait_ge(s.acc_read, sec * 48 + i * 4 + (2 * g + 2))
                        pool.tensor_copy(ff_tail[:, ds(sec * 16 + i * 2, 2), :], gs[:, :, S - 2:T])\
                            .then_inc(s.tail_saved, 1)

            def send(n):
                pool.wait_ge(s.out_rows, n + 1)
                for dst, r, m in plan[n][2]:
                    pool.dma_start(dst, row_slot(n)[r:r + m, 0:row_width(plan[n][0])]).then_inc(s.out_sent[n % 2], 16)

            ffn(0, CS_FFN0, 8, 32)
            for n in range(len(mid)):
                send(n)
            ffn(1, CS_FFN1, 32, 64)
            for n in range(len(mid), len(plan)):
                send(n)
            pool.wait_ge(s.shifted, 32)
            for n in (len(plan) - 2, len(plan) - 1):
                pool.wait_ge(s.out_sent[n % 2], out_sems[n])

        def split_width(c):
            return P if C_DKV + 8 <= c < C_DQ else 256

        @block.scalar
        def _(act):
            def split(c, off=0):
                act.wait_ge(s.raw_loaded[c % RAW], (off * 2) + loaded(c))
                if c >= SPLIT:
                    act.wait_ge(s.chunk_used, off + (c - SPLIT + 1))
                n = split_width(c)
                act.activation(hi[:, c % SPLIT, :, 0:n], raw[:, c % RAW, :, 0:n], ACT.Copy).then_inc(s.hi_ready, 1)

            def high_pair(src, done, tile):
                for m in range(2):
                    act.wait_ge(s.h_full, done + (m + 1))
                    act.activation(hh[:, ds(tile + m, 1), :], src[:, m:m + 1, :], ACT.Copy).then_inc(s.h_hi, 1)

            def norm(n, src, sq_to, tiles, out):
                step = 4
                for j in range(0, tiles, step):
                    last = act.activation(sq_to[:, j:j + step, :], src[:, j:j + step, :], ACT.Square)
                last.then_inc(s.sq_done, 1)

            def root(n, out):
                act.wait_ge(s.mean_step, 2 * n + 2)
                act.activation(out[:, :], mean[:, :], ACT.Sqrt).then_inc(s.rstd_ready, 1)

            def scaled(dst, base, xt, xn):
                for j in range(KT):
                    act.wait_ge(s.x_tile, xt + j + 1)
                    act.activation(dst[:, j, :], x[:, j, :], ACT.Copy, scale=PT[:, base + j:base + j + 1])\
                        .then_inc(s.xn_hi, 1)

            act.dma_start(xrows[:, :, :], I["x_prompt"][0].rearrange("(t p) d -> p t d", p=P)).then_inc(s.x_in, 16)
            act.dma_start(xsrows[:, :], I["x_sample"][:, 0, :]).then_inc(s.x_in, 16)
            for c in range(4):
                split(c)
            for n in range(6):
                act.wait_ge(s.turned, n + 1)
                w = min(512, PT_END - 512 * n)
                act.activation(PT[:, 512 * n:512 * n + w], mis[n % 4][:, 0:w], ACT.Copy).then_inc(s.pt_ready, 1)
            act.wait_ge(s.pt_ready, 6)
            act.activation(soft[:, 0, :], PT[:, PT_GATE + 2 * KT:PT_GATE + 3 * KT], ACT.Abs).then_inc(s.par_step, 1)
            act.wait_ge(s.par_step, 1)
            act.activation(soft[:, 1, :], soft[:, 0, :], ACT.Exp, scale=-1.0).then_inc(s.par_step, 1)
            act.wait_ge(s.pt_ready, 6)
            scaled(xnh, PT_NORM, 0, 0)
            norm(N_X0, x, sq_h, KT, rx)
            root(N_X0, rx)
            with act.Fori(0, 4) as i:
                for c in range(8):
                    split(C_RGX + 4 + c, off=i * 8)
            with act.Fori(0, 4) as i:
                for a in range(2):
                    act.wait_ge(s.gates, i * 2 + (a + 1))
                    act.wait_ge(s.gate_par, i * 2 + (a + 1))
                    act.wait_ge(s.gate_step, i * 20 + 10 * a)
                    for m in range(2):
                        act.activation(ta[:, m, :], mis[m][:, 0:T], ACT.Tanh, scale=0.5, bias=gp[:, 0, m:m + 1])\
                            .then_inc(s.gate_tanh, 1)
                    for m in range(2):
                        act.activation(ti[:, m, :], mis[2 + m][:, 0:T], ACT.Tanh, scale=0.5,
                                       bias=gp[:, 1, m:m + 1]).then_inc(s.gate_tanh, 1)
                    for m in range(2):
                        act.wait_ge(s.gate_tanh, i * 8 + (4 * a + m + 1))
                        act.activation(ta[:, m, :], ta[:, m, :], ACT.Tanh, scale=gp[:, 2, m:m + 1],
                                       bias=gp[:, 2, m:m + 1]).then_inc(s.gate_th, 1)
                    act.wait_ge(s.gate_th, i * 6 + (3 * a + 2))
                    act.activation(sq[:, :, :], ta[:, :, :], ACT.Sqrt).then_inc(s.gate_th, 1)
                    for c in range(4):
                        split(C_RGY + 4 + 4 * a + c, off=i * 8)
                    act.wait_ge(s.h_ready, i * 4 + 2 * a)
                    for m in range(2):
                        act.wait_ge(s.acc_read, i * 4 + (2 * a + 2 * G_RGY + m + 1))
                        act.activation(ge[:, m, :], gs[:, m, :], ACT.Gelu_apprx_tanh).then_inc(s.gelu_done, 1)
                    high_pair(ge, i * 4 + 2 * a, i * 4 + 2 * a)
            with act.Fori(0, 4) as i:
                for c in range(8):
                    split(C_RGO + 4 + c, off=i * 8)

            def boundary(b, n_f, n_x, acc_done, gains):
                act.wait_ge(s.acc_read, acc_done)
                norm(n_f, f, sq_xn, KT, rf)
                root(n_f, rf)
                if not gains:
                    return
                scaled(xnh, gains[0], 16 * (b + 1), 0)
                norm(n_x, x, sq_h, KT, rx)
                root(n_x, rx)
                if len(gains) > 1:
                    scaled(hh, gains[1], 16 * (b + 1), 0)

            def section(l, c0, h0, sec, last):
                with act.Fori(0, 8) as i:
                    for c in range(4):
                        split(c0 + 4 + c, off=sec * 96 + i * 8)
                    act.wait_ge(s.conv_step, sec * 80 + i * 10 + ((CS_FFN0, CS_FFN1)[l] + 10))
                    for m in range(2):
                        act.activation(ge[:, m, :], cv[:, m, :], ACT.Gelu_apprx_tanh).then_inc(s.gelu_done, 1)
                    for c in range(4):
                        split(c0 + 8 + c, off=sec * 96 + i * 8)
                    high_pair(us, sec * 16 + i * 2 + h0, i * 2)
                with act.Fori(0, 3 if last else 4) as i:
                    for c in range(8):
                        split(c0 + 68 + c, off=sec * 96 + i * 8)
                if last:
                    for c in range(4):
                        split(c0 + 68 + c, off=sec * 96 + 24)

            def ffn(l, c0, h0):
                with act.Fori(0, SECTIONS - 1) as sec:
                    section(l, c0, h0, sec, False)
                section(l, c0, h0, SECTIONS - 1, l == 1)

            boundary(0, N_RGO, N_X1, 2 * G_FFN0, [PT_NORM + 2 * KT])
            ffn(0, C_FFN0, H_FFN0)
            boundary(1, N_F0, N_X2, 2 * G_DKV, [PT_KVIN, PT_NORM + 4 * KT])
            for c in range(C_DKV + 4, C_DKV + 16):
                split(c)
            act.wait_ge(s.acc_read, 2 * G_DKV + 4)
            norm(N_C, pre, sqs, LT, rf)
            root(N_C, rf)
            for c in range(C_DQ + 4, C_DQ + 12):
                split(c)
            act.wait_ge(s.c_step, LT)
            act.activation(cTh[:, :, :], cT[:, :, :], ACT.Copy).then_inc(s.c_hi, 1)
            act.wait_ge(s.acc_read, 2 * G_UQ)
            norm(N_CQ, preq, sqs, LT, rf)
            root(N_CQ, rf)
            act.wait_ge(s.c_step, 2 * LT)
            act.activation(cqh[:, :, :], preq[:, :, :], ACT.Copy).then_inc(s.c_hi, 1)
            for c in range(C_UQ + 4, C_UQ + 16):
                split(c)

            def rows_out(n):
                act.wait_ge(s.out_turned, n + 1)
                if n >= 2:
                    act.wait_ge(s.out_sent[n % 2], out_sems[n - 2])
                tiles, m, _ = plan[n]
                w = row_width(tiles)
                act.activation(row_slot(n)[0:m, 0:w], mis[2 + n % 2][0:m, 0:w], ACT.Copy).then_inc(s.out_rows, 1)

            for n in range(len(mid)):
                rows_out(n)
            act.wait_ge(s.cn_turned, 1)
            act.activation(cnew[:, :], mis[0][0:NB, :], ACT.Copy).then_inc(s.cn_ready, 1)
            act.wait_ge(s.sh_done, 1)
            shifted = mis[1][0:ROPE, 0:NB * H // 2].rearrange("p (g b) -> p b g", b=NB)
            heads = qrs[:, :, :].rearrange("p b (g e) -> p b g e", e=2)
            act.activation(heads[:, :, :, 1], shifted, ACT.Copy).then_inc(s.sh_ready, 1)
            act.activation(heads[:, :, :, 0], qr[0:ROPE, :, S:T].rearrange("p g b -> p b g"), ACT.Copy)\
                .then_inc(s.sh_ready, 1)
            for u in range(8):
                split(C_UK + 4 + u)
                for m in range(2):
                    h = 2 * u + m
                    act.wait_ge(s.uk_turned, h + 1)
                    if u >= 1:
                        act.wait_ge(s.ql_done, h - 1)
                    act.activation(ukT[:, m, :], mis[m][:, :], ACT.Copy).then_inc(s.uk_read, 1)
                for m in range(2):
                    h = 2 * u + m
                    act.wait_ge(s.ql_done, h + 1)
                    src = mis[2 + m][:, 0:LT * NB].rearrange("p (c b) -> p c b", b=NB)
                    act.activation(qlat[:, :, :, h], src, ACT.Copy).then_inc(s.ql_ready, 1)
            act.wait_ge(s.ql_ready, H)
            act.wait_ge(s.sh_ready, 2)
            with act.Fori(0, NB // 2) as i:
                for a in range(2):
                    act.wait_ge(s.s_scored, i * 2 + a)
                    act.activation(qb[:, :, :], qlat[:, :, ds(i * 2 + a, 1), :].rearrange("p c a h -> p c (a h)"),
                                   ACT.Copy).then_inc(s.qb_ready, 1)
                    act.activation(qrb[:, :], qrs[:, ds(i * 2 + a, 1), :].rearrange("p a h -> p (a h)"),
                                   ACT.Copy).then_inc(s.qb_ready, 1)
                    for g in range(PAGES):
                        act.wait_ge(s.pg_turned, i * 16 + (8 * a + g + 1))
                        act.activation(ctp[:, g % 2, :, :].rearrange("p c k -> p (c k)"), acc[g % 2][:, :],
                                       ACT.Copy).then_inc(s.pg_c, 1)
                    act.wait_ge(s.s_step, i * 12 + (6 * a + 5))
                    act.activation(sp_[:, :], sp_[:, :], ACT.Exp, scale=ATTN_SCALE, bias=stats[0:H, 1:2],
                                   accum_out=stats[0:H, 2:3]).then_inc(s.s_exp, 1)
                    act.wait_ge(s.s_turned, i * 2 + (a + 1))
                    act.activation(spT[:, 0:PAGES, :].rearrange("p g h -> p (g h)"), mis[2][:, 0:PAGES * H],
                                   ACT.Copy).then_inc(s.s_pT, 1)
                    act.activation(spT[0:NB, PAGES, :], mis[2][0:NB, PAGES * H:(PAGES + 1) * H],
                                   ACT.Copy).then_inc(s.s_pT, 1)

            def exps(h):
                k = h % 2
                act.wait_ge(s.sm_step, 6 * h + 5)
                act.activation(sm[:, k, 0:P], sm[:, k, 0:P], ACT.Exp, scale=ATTN_SCALE,
                               bias=stats[:, 8 * k + 2:8 * k + 3],
                               accum_out=stats[:, 8 * k + 4:8 * k + 5]).then_inc(s.sm_exp, 1)
                act.activation(sm[:, k, P:3 * P], sm[:, k, P:3 * P], ACT.Exp, scale=ATTN_SCALE,
                               bias=stats[:, 8 * k + 3:8 * k + 4],
                               accum_out=stats[:, 8 * k + 5:8 * k + 6]).then_inc(s.sm_exp, 1)

            split(C_UV + 4)
            exps(0)
            for h in range(H):
                if h % 2 == 0 and h + 2 < H:
                    split(C_UV + 5 + h // 2)
                act.wait_ge(s.p_turned, h + 1)
                if h >= 1:
                    act.wait_ge(s.o_ps, h)
                act.activation(pTs[:, :], mis[2][:, 0:3 * P], ACT.Copy).then_inc(s.pT_ready, 1)
                if h + 1 < H:
                    exps(h + 1)
                act.wait_ge(s.o_ps, h + 1)
                act.activation(hh[:, h, :], mis[3][:, 0:T], ACT.Copy).then_inc(s.o_hi, 1)
            with act.Fori(0, 4) as i:
                for c in range(8):
                    split(C_MO + 4 + c, off=i * 8)
            boundary(2, N_MO, N_X3, 2 * G_FFN1, [PT_NORM + 6 * KT])
            ffn(1, C_FFN1, H_FFN1)
            boundary(3, N_F1, None, 2 * G_END, [])
            for n in range(len(mid), len(plan)):
                rows_out(n)

        @block.vector
        def _(dve):
            def split(c, off=0):
                dve.wait_ge(s.hi_ready, off + (c + 1))
                n = split_width(c)
                dve.tensor_tensor(lo[:, c % SPLIT, :, 0:n], raw[:, c % RAW, :, 0:n],
                                  hi[:, c % SPLIT, :, 0:n].bitcast(F32), ALU.subtract).then_inc(s.lo_ready, 1)

            par = [0]

            def par_op(ins):
                par[0] += 1
                ins.then_inc(s.par_step, 1)
                dve.wait_ge(s.par_step, par[0])

            def mean_square(n, sq_from, tiles, features):
                dve.wait_ge(s.sq_done, n + 1)
                dve.tensor_reduce(ssum[:, :], sq_from[:, :, :].rearrange("p j t -> p t j"), AX.X, ALU.add)\
                    .then_inc(s.sum_ready, 1)
                dve.wait_ge(s.stat_ready, n + 1)
                dve.tensor_scalar(mean[:, :], mis[3][:, 0:T], 1.0 / features, EPS, ALU.mult, ALU.add)\
                    .then_inc(s.mean_step, 1)
                dve.wait_ge(s.mean_step, 2 * n + 1)
                dve.reciprocal(mean[:, :], mean[:, :]).then_inc(s.mean_step, 1)

            def low(dst, dst_hi, base, j, n):
                dve.wait_ge(s.xn_hi, n + j + 1)
                dve.scalar_tensor_tensor(out=dst[:, j, :], in0=x[:, j, :], scalar=PT[:, base + j:base + j + 1],
                                         in1=dst_hi[:, j, :].bitcast(F32), op0=ALU.mult, op1=ALU.subtract)\
                    .then_inc(s.xn_ready, 1)

            def evac(ins):
                ins.then_inc(s.acc_read, 1)

            def low_pair(src, done, tile):
                for m in range(2):
                    dve.wait_ge(s.h_hi, done + (m + 1))
                    dve.tensor_tensor(hl[:, ds(tile + m, 1), :], src[:, m:m + 1, :],
                                      hh[:, ds(tile + m, 1), :].bitcast(F32), ALU.subtract).then_inc(s.h_ready, 1)

            def conv_pair(src, dst, taps, cw, done):
                k_state = taps - 1
                w = NB * k_state
                steps = []
                for k in range(k_state, -1, -1):
                    if k == k_state:
                        steps.append(("now", k, 0))
                        continue
                    steps.append(("past", k, k_state - k))
                    steps.append(("state", k, 0))
                for n, (kind, k, lag) in enumerate(steps):
                    for m in range(2):
                        wk = cw[:, w + k, m:m + 1]
                        if n:
                            dve.wait_ge(s.conv_step, done + (2 * (n - 1) + m + 1))
                        if kind == "now":
                            ins = dve.tensor_scalar(dst(m, 0, T), src[:, m, :], wk, cw[:, w + taps, m:m + 1],
                                                    ALU.mult, ALU.add)
                        elif kind == "past":
                            ins = dve.scalar_tensor_tensor(out=dst(m, lag, S), in0=src[:, m, 0:S - lag], scalar=wk,
                                                           in1=dst(m, lag, S), op0=ALU.mult, op1=ALU.add)
                        else:
                            ins = dve.scalar_tensor_tensor(out=dst(m, S, T), in0=cw[:, k:w:k_state, m], scalar=wk,
                                                           in1=dst(m, S, T), op0=ALU.mult, op1=ALU.add)
                        ins.then_inc(s.conv_step, 1)

            dve.memset(ones[:, :], 1.0).then_inc(s.ones_set, 1)
            for c in range(4):
                split(c)
            lam = PT[:, PT_GATE + 2 * KT:PT_GATE + 3 * KT]
            dve.wait_ge(s.pt_ready, 6)
            dve.wait_ge(s.par_step, 2)
            par[0] = 2
            par_op(dve.tensor_scalar(soft[:, 2, :], soft[:, 1, :], 2.0, None, ALU.add))
            par_op(dve.reciprocal(soft[:, 2, :], soft[:, 2, :]))
            par_op(dve.tensor_tensor(soft[:, 3, :], soft[:, 1, :], soft[:, 2, :], ALU.mult))
            par_op(dve.tensor_tensor(soft[:, 2, :], soft[:, 3, :], soft[:, 3, :], ALU.mult))
            par_op(dve.tensor_scalar(soft[:, 1, :], soft[:, 2, :], 1.0 / 17, None, ALU.mult))
            for k in (15, 13, 11, 9, 7, 5, 3):
                par_op(dve.scalar_tensor_tensor(out=soft[:, 1, :], in0=soft[:, 1, :], scalar=1.0 / k,
                                                in1=soft[:, 2, :], op0=ALU.add, op1=ALU.mult))
            par_op(dve.scalar_tensor_tensor(out=soft[:, 1, :], in0=soft[:, 1, :], scalar=1.0,
                                            in1=soft[:, 3, :], op0=ALU.add, op1=ALU.mult))
            par_op(dve.tensor_scalar(soft[:, 0, :], lam, -1.0, 0.0, ALU.mult, ALU.max))
            par_op(dve.scalar_tensor_tensor(out=soft[:, 1, :], in0=soft[:, 1, :], scalar=2.0,
                                            in1=soft[:, 0, :], op0=ALU.mult, op1=ALU.add))
            par_op(dve.tensor_scalar(lam, soft[:, 1, :], RG_C / 4, None, ALU.mult))
            par_op(dve.tensor_scalar(PT[:, PT_GATE:PT_GATE + 2 * KT], PT[:, PT_GATE:PT_GATE + 2 * KT], 0.5, None,
                                     ALU.mult))
            assert par[0] == PAR_STEPS
            for j in range(KT):
                dve.wait_ge(s.turned, 6 + j + 1)
                dve.tensor_copy(x[:, j, :], mis[(6 + j) % 4][:, 0:T]).then_inc(s.x_tile, 1)
            for j in range(KT):
                low(xnl, xnh, PT_NORM, j, XN_0)
            mean_square(N_X0, sq_h, KT, D)

            dve.wait_ge(s.rstd_ready, N_X0 + 1)
            with dve.Fori(0, 4) as i:
                for a in range(2):
                    for c in range(4):
                        split(C_RGX + 4 + 4 * a + c, off=i * 8)
                    dve.wait_ge(s.chunk_used, i * 8 + (C_RGX + 4 * a + 4))
                    dve.wait_ge(s.tail_saved, i * 2 + a)
                    for m in range(2):
                        evac(dve.tensor_tensor(gs[:, m, :], acc[2 * a + m][:, 0:T], rx[:, :], ALU.mult))
                    dve.wait_ge(s.cw_ready, i * 2 + (a + 1))
                    dve.wait_ge(s.acc_read, i * 4 + (2 * a + 2))

                    def f_tile(m, u, v, i=i, a=a):
                        return f[:, ds(i * 4 + (2 * a + m), 1), u:v].rearrange("p a t -> p (a t)")

                    conv_pair(gs, f_tile, 4, cwr, i * 28 + 14 * a)

            with dve.Fori(0, 4) as i:
                for a in range(2):
                    tile = i * 4 + 2 * a
                    step0 = i * 20 + 10 * a

                    def step(ins):
                        ins.then_inc(s.gate_step, 1)

                    dve.wait_ge(s.gate_th, i * 6 + (3 * a + 2))
                    step(dve.tensor_scalar(r1[:, :, :], ta[:, :, :], 1.0, None, ALU.add))
                    dve.wait_ge(s.gate_step, step0 + 1)
                    step(dve.reciprocal(r1[:, :, :], r1[:, :, :]))
                    dve.wait_ge(s.gate_step, step0 + 2)
                    step(dve.tensor_scalar(aa[:, :, :], r1[:, :, :], 2.0, -1.0, ALU.mult, ALU.add))
                    step(dve.scalar_tensor_tensor(out=ti[:, :, :], in0=ti[:, :, :], scalar=1.0,
                                                  in1=f[:, ds(tile, 2), :], op0=ALU.add, op1=ALU.mult))
                    dve.wait_ge(s.gate_step, step0 + 4)
                    step(dve.tensor_tensor(ti[:, :, :], ti[:, :, :], r1[:, :, :], ALU.mult))
                    dve.wait_ge(s.gate_step, step0 + 5)
                    dve.wait_ge(s.gate_th, i * 6 + (3 * a + 3))
                    step(dve.tensor_tensor(ti[:, :, :], ti[:, :, :], sq[:, :, :], ALU.mult))
                    h0 = gp[:, 3:3 + NB, :].rearrange("p b m -> p m b")
                    step(dve.tensor_tensor(aa[:, :, S:T], aa[:, :, S:T], h0, ALU.mult))
                    dve.wait_ge(s.gate_step, step0 + 7)
                    for m in range(2):
                        step(dve.tensor_tensor_scan(
                            f[:, ds(tile + m, 1), 0:S].rearrange("p a t -> p (a t)"), aa[:, m, 0:S],
                            ti[:, m, 0:S], 0.0, ALU.mult, ALU.add))
                    step(dve.tensor_tensor(f[:, ds(tile, 2), S:T], aa[:, :, S:T], ti[:, :, S:T], ALU.add))
                    for c in range(4):
                        split(C_RGY + 4 + 4 * a + c, off=i * 8)
                    dve.wait_ge(s.chunk_used, i * 8 + (C_RGY + 4 * a + 4))
                    dve.wait_ge(s.gate_step, step0 + 10)
                    for m in range(2):
                        evac(dve.tensor_tensor(gs[:, m, :], acc[2 * a + m][:, 0:T], rx[:, :], ALU.mult))
                    for m in range(2):
                        dve.wait_ge(s.gelu_done, tile + (m + 1))
                        dve.tensor_tensor(ge[:, m:m + 1, :], ge[:, m:m + 1, :], f[:, ds(tile + m, 1), :], ALU.mult)\
                            .then_inc(s.h_full, 1)
                    low_pair(ge, tile, tile)
            dve.wait_ge(s.ht_saved, 8)
            def project(c0, g0):
                with dve.Fori(0, 4) as i:
                    for a in range(2):
                        for c in range(4):
                            split(c0 + 4 + 4 * a + c, off=i * 8)
                        dve.wait_ge(s.chunk_used, i * 8 + (c0 + 4 * a + 4))
                        for m in range(2):
                            evac(dve.tensor_copy(f[:, ds(i * 4 + (2 * a + m), 1), :].rearrange("p a t -> p (a t)"),
                                                 acc[(2 * (g0 + a) + m) % 4][:, 0:T]))

            def boundary(b, l, g_out, n_f, n_x, gains):
                mean_square(n_f, sq_xn, KT, D)
                dve.wait_ge(s.rstd_ready, n_f + 1)
                xt = 16 * (b + 1)

                def add(j):
                    dve.wait_ge(s.fnorm, 16 * b + j + 1)
                    dve.tensor_tensor(x[:, j, :], x[:, j, :], f[:, j, :], ALU.add).then_inc(s.x_tile, 1)

                for j in range(KT):
                    base = PT_NORM + (4 * l + g_out) * KT + j
                    dve.scalar_tensor_tensor(out=f[:, j, :], in0=f[:, j, :], scalar=PT[:, base:base + 1],
                                             in1=rf[:, :], op0=ALU.mult, op1=ALU.mult).then_inc(s.fnorm, 1)
                    if j >= 1:
                        add(j - 1)
                    if j >= 3 and gains:
                        low(xnl, xnh, gains[0][0], j - 3, gains[0][1])
                add(KT - 1)
                if not gains:
                    return
                for j in range(KT - 3, KT):
                    low(xnl, xnh, gains[0][0], j, gains[0][1])
                mean_square(n_x, sq_h, KT, D)
                if len(gains) > 1:
                    for j in range(KT):
                        low(hl, hh, gains[1][0], j, gains[1][1])
                dve.wait_ge(s.rstd_ready, n_x + 1)

            def section(l, c0, g0, h0, sec, last):
                with dve.Fori(0, 8) as i:
                    off = sec * 96 + i * 8
                    acc_g, acc_u = 2 * (g0 % 2), 2 * ((g0 + 1) % 2)
                    for c in range(4):
                        split(c0 + 4 + c, off=off)
                    dve.wait_ge(s.chunk_used, off + (c0 + 4))
                    dve.wait_ge(s.tail_saved, sec * 8 + i + (8, 32)[l])
                    for m in range(2):
                        evac(dve.tensor_tensor(gs[:, m, :], acc[acc_g + m][:, 0:T], rx[:, :], ALU.mult))
                    dve.wait_ge(s.cw_ready, sec * 8 + i + (9, 33)[l])
                    dve.wait_ge(s.acc_read, sec * 48 + i * 4 + (2 * g0 + 2))
                    conv_pair(gs, lambda m, u, v: cv[:, m, u:v], 3, cwf, sec * 80 + i * 10 + (CS_FFN0, CS_FFN1)[l])
                    for c in range(4):
                        split(c0 + 8 + c, off=off)
                    dve.wait_ge(s.chunk_used, off + (c0 + 8))
                    for m in range(2):
                        evac(dve.tensor_tensor(us[:, m, :], acc[acc_u + m][:, 0:T], rx[:, :], ALU.mult))
                    for m in range(2):
                        dve.wait_ge(s.gelu_done, sec * 16 + i * 2 + (h0 + m + 1))
                        dve.wait_ge(s.acc_read, sec * 48 + i * 4 + (2 * g0 + 3 + m))
                        dve.tensor_tensor(us[:, m, :], us[:, m, :], ge[:, m, :], ALU.mult).then_inc(s.h_full, 1)
                    low_pair(us, sec * 16 + i * 2 + h0, i * 2)
                dve.wait_ge(s.f_zero, l + 1)

                def down(i, leads):
                    for a in range(2):
                        if a in leads:
                            for c in range(4):
                                split(c0 + 68 + 4 * a + c, off=sec * 96 + i * 8)
                        dve.wait_ge(s.chunk_used, sec * 96 + i * 8 + (c0 + 64 + 4 * a + 4))
                        for m in range(2):
                            ft = f[:, ds(i * 4 + (2 * a + m), 1), :].rearrange("p a t -> p (a t)")
                            evac(dve.tensor_tensor(ft, acc[(2 * (g0 + a) + m) % 4][:, 0:T], ft, ALU.add))

                with dve.Fori(0, 3 if last else 4) as i:
                    down(i, (0, 1))
                if last:
                    down(3, (0,))

            def ffn(l, c0, g0, h0):
                with dve.Fori(0, SECTIONS - 1) as sec:
                    section(l, c0, g0, h0, sec, False)
                section(l, c0, g0, h0, SECTIONS - 1, l == 1)

            project(C_RGO, G_RGO)
            dve.wait_ge(s.acc_read, 2 * G_FFN0)
            boundary(0, 0, 1, N_RGO, N_X1, [(PT_NORM + 2 * KT, XN_1)])
            ffn(0, C_FFN0, G_FFN0, H_FFN0)
            dve.wait_ge(s.acc_read, 2 * G_DKV)
            boundary(1, 0, 3, N_F0, N_X2, [(PT_KVIN, XN_KV), (PT_NORM + 4 * KT, XN_Q)])

            def copies(g, dst, c_last, scale=True):
                dve.wait_ge(s.chunk_used, c_last + 1)
                for m in range(2):
                    src = acc[2 * (g % 2) + m][:, 0:T]
                    if scale:
                        evac(dve.tensor_tensor(dst(m), src, rx[:, :], ALU.mult))
                    else:
                        evac(dve.tensor_copy(dst(m), src))

            for a in range(2):
                for c in range(4):
                    split(C_DKV + 4 + 4 * a + c)
                copies(G_DKV + a, lambda m: pre[:, 2 * a + m, :], C_DKV + 4 * a + 3)
            for c in range(4):
                split(C_DKV + 12 + c)
            dve.wait_ge(s.chunk_used, C_DKV + 12)
            g = G_DKV + 2
            dve.tensor_tensor(prk[:, :], acc[2 * (g % 2)][:, 0:T], rx[:, :], ALU.mult).then_inc(s.acc_read, 2)
            mean_square(N_C, sqs, LT, LORA)
            for a in range(2):
                for c in range(4):
                    split(C_DQ + 4 + 4 * a + c)
                copies(G_DQ + a, lambda m: preq[:, 2 * a + m, :], C_DQ + 4 * a + 3)
            dve.wait_ge(s.rstd_ready, N_C + 1)
            dve.wait_ge(s.tail_saved, 32)
            for k in range(LT):
                dve.scalar_tensor_tensor(out=cT[:, k, :], in0=pre[:, k, :], scalar=PT[:, PT_KVN + k:PT_KVN + k + 1],
                                         in1=rf[:, :], op0=ALU.mult, op1=ALU.mult).then_inc(s.c_step, 1)
            dve.tensor_tensor(rot[:, 0, :], prk[:, :], cos_, ALU.mult).then_inc(s.kr_step, 1)
            dve.wait_ge(s.kr_rot, 1)
            dve.tensor_tensor(krT[:, :], mis[0][:, 0:T], sin_, ALU.mult).then_inc(s.kr_step, 1)
            dve.wait_ge(s.kr_step, 2)
            dve.tensor_tensor(krT[:, :], krT[:, :], rot[:, 0, :], ALU.add).then_inc(s.kr_step, 1)
            dve.wait_ge(s.c_hi, 1)
            dve.tensor_tensor(cTl[:, :, :], cT[:, :, :], cTh[:, :, :].bitcast(F32), ALU.subtract).then_inc(s.c_ready, 1)
            mean_square(N_CQ, sqs, LT, LORA)
            dve.wait_ge(s.rstd_ready, N_CQ + 1)
            for k in range(LT):
                dve.scalar_tensor_tensor(out=preq[:, k, :], in0=preq[:, k, :], scalar=PT[:, PT_QN + k:PT_QN + k + 1],
                                         in1=rf[:, :], op0=ALU.mult, op1=ALU.mult).then_inc(s.c_step, 1)
            dve.wait_ge(s.c_hi, 2)
            dve.tensor_tensor(cql[:, :, :], preq[:, :, :], cqh[:, :, :].bitcast(F32), ALU.subtract)\
                .then_inc(s.c_ready, 1)

            def rope(j):
                dve.wait_ge(s.q_rot, j + 1)
                dve.tensor_tensor(rot[:, j % 2, :], qr[:, j, :], cos_, ALU.mult).then_inc(s.q_step, 1)
                dve.wait_ge(s.q_step, 3 * j + 1)
                dve.tensor_tensor(qr[:, j, :], mis[j % 2][:, 0:T], sin_, ALU.mult).then_inc(s.q_step, 1)
                dve.wait_ge(s.q_step, 3 * j + 2)
                dve.tensor_tensor(qr[:, j, :], qr[:, j, :], rot[:, j % 2, :], ALU.add).then_inc(s.q_step, 1)

            for g4 in range(4):
                for e in range(3):
                    c = C_UQ + 3 * g4 + e
                    split(c + 4)
                    if e < 2:
                        copies(G_UQ + 3 * g4 + e, lambda m: qn[:, 4 * g4 + 2 * e + m, :], c, False)
                    else:
                        copies(G_UQ + 3 * g4 + e, lambda m: qr[:, 2 * g4 + m, :], c, False)
                    if e == 0 and g4:
                        rope(2 * g4 - 2)
                        rope(2 * g4 - 1)
            rope(6)
            rope(7)
            for u in range(8):
                split(C_UK + 4 + u)
                dve.wait_ge(s.chunk_used, C_UK + u + 1)
                for m in range(2):
                    evac(dve.tensor_copy(kn[:, 2 * u + m, :], acc[2 * ((G_UK + u) % 2) + m][:, 0:S]))

            with dve.Fori(0, NB // 2) as i:
                for a in range(2):
                    for g in range(PAGES):
                        dve.wait_ge(s.pg_turned, i * 16 + (8 * a + g + 1))
                        dve.tensor_copy(krp[:, g % 2, :], acc[2 + g % 2][0:ROPE, 0:P]).then_inc(s.pg_k, 1)
                    st = i * 12 + 6 * a
                    dve.wait_ge(s.s_scored, i * 2 + (a + 1))
                    dve.tensor_copy(sp_[:, 0:512], mis[0][0:H, :]).then_inc(s.s_step, 1)
                    dve.tensor_copy(sp_[:, 512:1024], mis[1][0:H, :]).then_inc(s.s_step, 1)
                    own = kc[0:H, ds(i * 2 * NB + (K_OWN + a * NB), NB)]
                    dve.tensor_tensor(sp_[:, 1024:KEYS], mis[2][0:H, 0:NB], own, ALU.add).then_inc(s.s_step, 1)
                    dve.wait_ge(s.s_step, st + 3)
                    dve.tensor_reduce(stats[0:H, 0:1], sp_[:, :], AX.X, ALU.max).then_inc(s.s_step, 1)
                    dve.wait_ge(s.s_step, st + 4)
                    dve.tensor_scalar(stats[0:H, 1:2], stats[0:H, 0:1], -ATTN_SCALE, None, ALU.mult)\
                        .then_inc(s.s_step, 1)
                    dve.wait_ge(s.s_exp, i * 2 + (a + 1))
                    dve.reciprocal(stats[0:H, 3:4], stats[0:H, 2:3]).then_inc(s.s_step, 1)
                    dve.wait_ge(s.s_step, st + 6)
                    dve.tensor_scalar(sp_[:, :], sp_[:, :], stats[0:H, 3:4], None, ALU.mult).then_inc(s.s_prob, 1)
                    dve.wait_ge(s.s_out, i * 2 + (a + 1))
                    dve.tensor_copy(olat[:, :, :, ds(i * 2 + a, 1)].rearrange("p c h b -> p (c h b)"),
                                    mis[3][:, 0:LT * H]).then_inc(s.ol_ready, 1)

            def soft_a(h):
                k = h % 2
                sc = mis[k]
                dve.wait_ge(s.scored, h + 1)
                diag = sm[:, k, :].rearrange("p (b q) -> p b q", q=P)[:, 0:3:2, :]
                dps = sc[:, 0:3 * P].rearrange("p (b q) -> p b q", q=P)[:, 0:3:2, :]
                mk = mask.rearrange("p (a q) -> p a q", a=1).to_broadcast([P, 2, P])
                dve.tensor_tensor(diag, dps, mk, ALU.add).then_inc(s.sm_step, 1)
                dve.tensor_copy(sm[:, k, P:2 * P], sc[:, P:2 * P]).then_inc(s.sm_step, 1)
                dve.wait_ge(s.sm_step, 6 * h + 2)
                dve.tensor_reduce(stats[:, 8 * k:8 * k + 1], sm[:, k, 0:P], AX.X, ALU.max).then_inc(s.sm_step, 1)
                dve.tensor_reduce(stats[:, 8 * k + 1:8 * k + 2], sm[:, k, P:3 * P], AX.X, ALU.max)\
                    .then_inc(s.sm_step, 1)
                dve.wait_ge(s.sm_step, 6 * h + 4)
                dve.tensor_scalar(stats[:, 8 * k + 2:8 * k + 4], stats[:, 8 * k:8 * k + 2], -ATTN_SCALE, None,
                                  ALU.mult).then_inc(s.sm_step, 1)

            def values(u):
                split(C_UV + 4 + u)
                dve.wait_ge(s.chunk_used, C_UV + u + 1)
                if u >= 2:
                    dve.wait_ge(s.o_ps, 2 * (u - 1))
                for m in range(2):
                    evac(dve.tensor_copy(Vs[:, u % 2, m, :], acc[2 * ((G_UV + u) % 2) + m][:, 0:256]))

            values(0)
            soft_a(0)
            for h in range(H):
                k = h % 2
                if k == 0 and h + 2 < H:
                    values(h // 2 + 1)
                dve.wait_ge(s.sm_exp, 2 * h + 2)
                dve.reciprocal(stats[:, 8 * k + 6:8 * k + 8], stats[:, 8 * k + 4:8 * k + 6]).then_inc(s.sm_step, 1)
                dve.wait_ge(s.sm_step, 6 * h + 6)
                for q, (u, v) in enumerate(((0, P), (P, 3 * P))):
                    dve.tensor_scalar(sm[:, k, u:v], sm[:, k, u:v], stats[:, 8 * k + 6 + q:8 * k + 7 + q], None,
                                      ALU.mult).then_inc(s.prob, 1)
                if h + 1 < H:
                    soft_a(h + 1)
                dve.wait_ge(s.o_hi, h + 1)
                dve.tensor_tensor(hl[:, h, :], mis[3][:, 0:T], hh[:, h, :].bitcast(F32), ALU.subtract)\
                    .then_inc(s.o_ready, 1)
            project(C_MO, G_MO)
            dve.wait_ge(s.acc_read, 2 * G_FFN1)
            boundary(2, 1, 1, N_MO, N_X3, [(PT_NORM + 6 * KT, XN_3)])
            ffn(1, C_FFN1, G_FFN1, H_FFN1)
            dve.wait_ge(s.acc_read, 2 * G_END)
            boundary(3, 1, 3, N_F1, None, [])

        @block.tensor
        def _(pe):
            def mm3(out, wh, wl, xh, xl, start, stop):
                pe.matmul(out, wh, xh, start=start, stop=False)
                pe.matmul(out, wh, xl, start=False, stop=False)
                return pe.matmul(out, wl, xh, start=False, stop=stop)

            def group(c, n, g, xh, xl, ready, g_off=0, c_off=0, tiles=2):
                if isinstance(g_off, int):
                    if g + g_off >= 2:
                        pe.wait_ge(s.acc_read, 2 * (g + g_off - 1))
                else:
                    pe.wait_ge(s.acc_read, g_off * 2 + 2 * (g - 1))
                for q in range(n):
                    ready(q)
                    pe.wait_ge(s.lo_ready, c_off + (c + q + 1))
                    slot = (c + q) % SPLIT
                    for m in range(tiles):
                        for k in range(4):
                            kk = 4 * q + k
                            w = (slice(None), slot, k, slice(m * P, m * P + P))
                            last = mm3(acc[2 * (g % 2) + m][:, 0:T], hi[w], lo[w], xh[:, kk, :], xl[:, kk, :],
                                       start=kk == 0, stop=kk == 4 * n - 1)
                    last.then_inc(s.chunk_used, 1)

            def stream(c0, g0, xh, xl, ready, first=0):
                if first:
                    for a in range(2):
                        group(c0 + 4 * a, 4, g0 + a, xh, xl, ready)
                with pe.Fori(first, 4) as i:
                    for a in range(2):
                        group(c0 + 4 * a, 4, g0 + a, xh, xl, ready, g_off=i * 2, c_off=i * 8)

            def xn(base):
                return lambda q: pe.wait_ge(s.xn_ready, base + 4 * (q + 1))

            def row_sum(n):
                pe.wait_ge(s.sum_ready, n + 1)
                pe.matmul(mis[3][:, 0:T], ones[:, :], ssum[:, :], start=True, stop=True).then_inc(s.stat_ready, 1)

            pe.wait_ge(s.const_in, 16)
            pe.wait_ge(s.rows_in, 16 * len(row_pieces))
            for n in range(6):
                if n >= 4:
                    pe.wait_ge(s.pt_ready, n - 3)
                for k in range(4 * n, min(4 * n + 4, PT_TILES)):
                    m = min(P, PT_END - P * k)
                    last = pe.transpose(mis[n % 4][:, P * (k % 4):P * (k % 4) + m], ptrows[0:m, k, :],
                                        ident[0:m, 0:m])
                last.then_inc(s.turned, 1)
            pe.wait_ge(s.x_in, 32)
            for j in range(KT):
                n = 6 + j
                if n < 10:
                    pe.wait_ge(s.pt_ready, n - 3)
                else:
                    pe.wait_ge(s.x_tile, n - 9)
                bank = mis[n % 4]
                for t in range(2):
                    pe.transpose(bank[:, P * t:P * t + P], xrows[:, t, P * j:P * j + P], ident)
                pe.transpose(bank[:, S:T], xsrows[:, P * j:P * j + P], ident[0:NB, 0:NB]).then_inc(s.turned, 1)
            pe.wait_ge(s.ones_set, 1)
            for a in range(2):
                group(4 * a, 4, a, xnh, xnl, xn(XN_0))
                if a == 0:
                    row_sum(N_X0)
            with pe.Fori(1, 4) as i:
                for a in range(2):
                    group(4 * a, 4, a, xnh, xnl, xn(XN_0), g_off=i * 2, c_off=i * 8)
            with pe.Fori(0, 4) as i:
                for a in range(2):
                    pe.wait_ge(s.gw_loaded[a], i * 32 + 32)
                    pe.wait_ge(s.conv_step, 14 * 8)
                    pe.wait_ge(s.gate_tanh, i * 8 + 4 * a)
                    for e in range(2):
                        for m in range(2):
                            for k in range(2):
                                last = pe.matmul(mis[2 * e + m][:, 0:T], gw[:, a, 2 * e + k, m * P:m * P + P],
                                                 f[:, ds(i * 4 + (2 * a + k), 1), :].rearrange("p a t -> p (a t)"),
                                                 start=k == 0, stop=k == 1)
                    last.then_inc(s.gates, 1)
                    group(C_RGY + 4 * a, 4, G_RGY + a, xnh, xnl, xn(XN_0), g_off=i * 2, c_off=i * 8)
            stream(C_RGO, G_RGO, hh, hl, lambda q: pe.wait_ge(s.h_ready, 4 * (q + 1)))

            def ffn(l, c0, g0, h0, xbase, n_x):
                def section(sec, first):
                    def pair_i(i):
                        group(c0, 4, g0, xnh, xnl, xn(xbase), g_off=sec * 24 + i * 2, c_off=sec * 96 + i * 8)
                        if first and isinstance(i, int):
                            row_sum(n_x)
                        group(c0 + 4, 4, g0 + 1, xnh, xnl, xn(xbase), g_off=sec * 24 + i * 2,
                              c_off=sec * 96 + i * 8)

                    if first:
                        pair_i(0)
                    with pe.Fori(1 if first else 0, 8) as i:
                        pair_i(i)
                    with pe.Fori(0, 4) as i:
                        for a in range(2):
                            group(c0 + 64 + 4 * a, 4, g0 + 16 + a, hh, hl,
                                  lambda q: pe.wait_ge(s.h_ready, sec * 16 + (h0 + 4 * (q + 1))),
                                  g_off=sec * 24 + i * 2, c_off=sec * 96 + i * 8)

                section(0, True)
                with pe.Fori(1, SECTIONS) as sec:
                    section(sec, False)

            row_sum(N_RGO)
            ffn(0, C_FFN0, G_FFN0, H_FFN0, XN_1, N_X1)
            row_sum(N_F0)
            group(C_DKV, 4, G_DKV, xnh, xnl, xn(XN_KV))
            row_sum(N_X2)
            group(C_DKV + 4, 4, G_DKV + 1, xnh, xnl, xn(XN_KV))
            group(C_DKV + 8, 4, G_DKV + 2, xnh, xnl, xn(XN_KV), tiles=1)
            row_sum(N_C)
            for a in range(2):
                group(C_DQ + 4 * a, 4, G_DQ + a, hh, hl, xn(XN_Q))
            pe.wait_ge(s.acc_read, 2 * G_DQ)
            pe.matmul(mis[0][:, 0:T], swap, prk[:, :], start=True, stop=True).then_inc(s.kr_rot, 1)
            row_sum(N_CQ)

            def rotate(j):
                pe.wait_ge(s.acc_read, 2 * (G_UQ + 3 * (j // 2) + 3))
                if j >= 2:
                    pe.wait_ge(s.q_step, 3 * (j - 1))
                else:
                    pe.wait_ge(s.kr_step, 3)
                pe.matmul(mis[j % 2][:, 0:T], swap, qr[:, j, :], start=True, stop=True).then_inc(s.q_rot, 1)

            for g4 in range(4):
                for e in range(3):
                    g = G_UQ + 3 * g4 + e
                    group(C_UQ + 3 * g4 + e, 1, g, cqh, cql, lambda q: pe.wait_ge(s.c_ready, 2))
                    if e == 0 and g4:
                        rotate(2 * g4 - 2)
                        rotate(2 * g4 - 1)
            pe.wait_ge(s.acc_read, 2 * G_UK)
            rotate(6)
            rotate(7)
            pe.wait_ge(s.q_step, 24)

            def turn_out(n):
                if n >= 2:
                    pe.wait_ge(s.out_rows, n - 1)
                tiles, m, _ = plan[n]
                col = 0
                for t in tiles:
                    w = t.shape[0]
                    last = pe.transpose(mis[2 + n % 2][0:m, col:col + w], t, ident[0:w, 0:w])
                    col += w
                last.then_inc(s.out_turned, 1)

            pe.wait_ge(s.tail_saved, 32)
            pe.wait_ge(s.ht_saved, 8)
            pe.wait_ge(s.c_step, LT)
            pe.wait_ge(s.kr_step, 3)
            for n in range(len(mid)):
                turn_out(n)
            for k in range(LT):
                last = pe.transpose(mis[0][0:NB, P * k:P * k + P], cT[:, k, S:T], ident)
            last.then_inc(s.cn_turned, 1)
            pe.matmul(mis[1][0:ROPE, 0:NB * H // 2], ident[:, ROPE:P], qr[:, :, S:T].rearrange("p g b -> p g b"),
                      start=True, stop=True).then_inc(s.sh_done, 1)
            pe.wait_ge(s.cn_ready, 1)
            pe.wait_ge(s.sh_ready, 1)
            pe.wait_ge(s.out_rows, len(mid))
            for u in range(8):
                c = C_UK + u
                pe.wait_ge(s.lo_ready, c + 1)
                for m in range(2):
                    if u >= 1:
                        pe.wait_ge(s.uk_read, 2 * u - 1 + m)
                    for k in range(4):
                        last = pe.transpose(mis[m][:, P * k:P * k + P], raw[:, c % RAW, k, P * m:P * m + P], ident)
                    last.then_inc(s.uk_turned, 1)
                pe.wait_ge(s.acc_read, 2 * (G_UK + u - 1))
                for m in range(2):
                    for k in range(4):
                        w = (slice(None), c % SPLIT, k, slice(m * P, m * P + P))
                        last = mm3(acc[2 * ((G_UK + u) % 2) + m][:, 0:S], hi[w], lo[w], cTh[:, k, 0:S],
                                   cTl[:, k, 0:S], start=k == 0, stop=k == 3)
                last.then_inc(s.chunk_used, 1)
                for m in range(2):
                    pe.wait_ge(s.uk_read, 2 * u + m + 1)
                    if u >= 1:
                        pe.wait_ge(s.ql_ready, 2 * u - 1 + m)
                    for k in range(4):
                        last = pe.matmul(mis[2 + m][:, NB * k:NB * k + NB], ukT[:, m, P * k:P * k + P],
                                         qn[:, 2 * u + m, S:T], start=True, stop=True)
                    last.then_inc(s.ql_done, 1)

            pe.wait_ge(s.acc_read, 2 * G_UV)
            pe.wait_ge(s.ql_ready, H)
            with pe.Fori(0, NB // 2) as i:
                for a in range(2):
                    def turn_page(g):
                        if g % 4 == 0:
                            pe.wait_ge(s.page_in[2 * a + g // 4], i * 128 + 128)
                        for k in range(LT):
                            pe.transpose(acc[g % 2][:, P * k:P * k + P],
                                         cpage[:, 2 * a + g // 4, g % 4, P * k:P * k + P], ident)
                        pe.transpose(acc[2 + g % 2][0:ROPE, 0:P], kpage[:, 2 * a + g // 4, g % 4, :], ident)\
                            .then_inc(s.pg_turned, 1)

                    def score_page(g):
                        pe.wait_ge(s.pg_c, i * 16 + (8 * a + g + 1))
                        pe.wait_ge(s.pg_k, i * 16 + (8 * a + g + 1))
                        out = mis[g // 4][0:H, P * (g % 4):P * (g % 4) + P]
                        for k in range(LT):
                            pe.matmul(out, qb[:, k, :], ctp[:, g % 2, k, :], start=k == 0, stop=False)
                        return pe.matmul(out, qrb[:, :], krp[:, g % 2, :], start=False, stop=True)

                    turn_page(0)
                    pe.wait_ge(s.qb_ready, i * 4 + (2 * a + 2))
                    for g in range(PAGES):
                        if g + 1 < PAGES:
                            turn_page(g + 1)
                        score_page(g)
                    new = mis[2][0:H, 0:NB]
                    for k in range(LT):
                        pe.matmul(new, qb[:, k, :], cT[:, k, S:T], start=k == 0, stop=False)
                    pe.matmul(new, qrb[:, :], krT[0:ROPE, S:T], start=False, stop=True).then_inc(s.s_scored, 1)
                    pe.wait_ge(s.s_prob, i * 2 + (a + 1))
                    pe.matmul(mis[2][:, 0:H], sp_[:, 0:P], ident[0:H, 0:H], start=True, stop=True)
                    for g in range(1, PAGES):
                        pe.transpose(mis[2][:, H * g:H * g + H], sp_[:, P * g:P * g + P], ident[0:H, 0:H])
                    pe.transpose(mis[2][0:NB, PAGES * H:PAGES * H + H], sp_[:, PAGES * P:KEYS], ident[0:H, 0:H])\
                        .then_inc(s.s_turned, 1)
                    pe.wait_ge(s.s_pT, i * 4 + (2 * a + 2))
                    pe.wait_ge(s.ol_ready, i * 2 + a)
                    for k in range(LT):
                        out = mis[3][:, H * k:H * k + H]
                        for g in range(PAGES):
                            pe.matmul(out, cpage[:, 2 * a + g // 4, g % 4, P * k:P * k + P], spT[:, g, :],
                                      start=g == 0, stop=False)
                        last = pe.matmul(out, cnew[:, P * k:P * k + P], spT[0:NB, PAGES, :], start=False, stop=True)
                    last.then_inc(s.s_out, 1)
            pe.wait_ge(s.ol_ready, NB)

            def value_pair(u):
                c, g = C_UV + u, G_UV + u
                pe.wait_ge(s.lo_ready, c + 1)
                pe.wait_ge(s.acc_read, 2 * (g - 1))
                for m in range(2):
                    for k in range(4):
                        keys = slice(m * P, m * P + P)
                        ah, al = cTh[:, k, keys], cTl[:, k, keys]
                        out = acc[2 * (g % 2) + m][:, 0:256]
                        last = mm3(out, ah, al, hi[:, c % SPLIT, k, :], lo[:, c % SPLIT, k, :], k == 0, k == 3)
                last.then_inc(s.chunk_used, 1)

            def scores(h):
                out = mis[h % 2]
                half = slice(ROPE * (h % 2), ROPE * (h % 2) + ROPE)
                for q in range(2):
                    o = out[:, P * q:P * q + P * (q + 1)]
                    pe.matmul(o, qn[:, h, P * q:P * q + P], kn[:, h, 0:P * (q + 1)], start=True, stop=False)
                    last = pe.matmul(o, qr[half, h // 2, P * q:P * q + P], krT[half, 0:P * (q + 1)],
                                     start=False, stop=True)
                last.then_inc(s.scored, 1)

            value_pair(0)
            scores(0)
            for h in range(H):
                k2 = h % 2
                if k2 == 0 and h + 2 < H:
                    value_pair(h // 2 + 1)
                if h + 1 < H:
                    scores(h + 1)
                pe.wait_ge(s.prob, 2 * h + 2)
                for b in range(3):
                    last = pe.transpose(mis[2][:, P * b:P * b + P], sm[:, k2, P * b:P * b + P], ident)
                last.then_inc(s.p_turned, 1)
                u = h // 2
                pe.wait_ge(s.pT_ready, h + 1)
                pe.wait_ge(s.acc_read, 2 * (G_UV + u + 1))
                if h >= 1:
                    pe.wait_ge(s.o_ready, h)
                v = slice(P * k2, P * k2 + P)
                pe.matmul(mis[3][:, 0:S], Vs[:, u % 2, 0, v], pTs[:, 0:S], start=True, stop=False,
                          skip_group_check=True)
                pe.matmul(mis[3][:, P:S], Vs[:, u % 2, 1, v], pTs[:, S:S + P], start=False, stop=False,
                          skip_group_check=True)
                for k in range(4):
                    last = pe.matmul(mis[3][:, S:T], raw[:, (C_UV + u) % RAW, k, v], olat[:, k, h, :], start=False,
                                     stop=k == 3, skip_group_check=True)
                last.then_inc(s.o_ps, 1)
            stream(C_MO, G_MO, hh, hl, lambda q: pe.wait_ge(s.o_ready, 4 * (q + 1)))
            row_sum(N_MO)
            ffn(1, C_FFN1, G_FFN1, H_FFN1, XN_3, N_X3)
            row_sum(N_F1)
            pe.wait_ge(s.tail_saved, 56)
            pe.wait_ge(s.mean_step, 2 * N_F1 + 1)
            for n in range(len(mid), len(plan)):
                if n == len(mid) + FT // 4:
                    pe.wait_ge(s.x_tile, 16 * 5)
                turn_out(n)


_INS = ["x_prompt", "x_sample", "state_rglru_h", "state_rglru_conv", "state_ffn_conv", "cache_kv_latent",
        "cache_k_rope", "page_table", "norm_g", "w_rg_in", "conv_rg_w", "conv_rg_b", "w_rg_a", "b_rg_a",
        "w_rg_i", "b_rg_i", "rg_lambda", "w_rg_o", "kv_in_g", "w_dkv", "kv_norm_g", "w_uk", "w_uv", "w_dq",
        "q_norm_g", "w_uq", "w_mla_o", "w_ffn_g", "w_ffn_u", "ffn_conv_w", "ffn_conv_b", "w_ffn_d"]
_OUTS = {"y_p": (1, S, D), "y_s": (NB, 1, D), "p_h": (1, 1, D), "s_h": (1, NB, D), "p_rgc": (1, 1, 3, D),
         "s_rgc": (1, NB, 3, D), "p_ffc": (2, 1, 2, FF), "s_ffc": (2, NB, 2, FF), "p_kv": (1, S, LORA),
         "s_kv": (NB, 1, LORA), "p_kr": (1, S, ROPE), "s_kr": (NB, 1, ROPE)}


def shape_constants():
    import numpy as np

    k = np.zeros((P, K_END), np.float32)
    k[:, K_ID:K_ID + P] = np.eye(P)
    half = ROPE // 2
    inv = np.float32(10000.0) ** (-np.arange(half, dtype=np.float32) * np.float32(2.0) / np.float32(ROPE))
    pos = np.concatenate([np.arange(S), np.full(NB, PAGES * PAGE)]).astype(np.float32)
    ang = (pos[None, :] * inv[np.arange(P) % half][:, None]).astype(np.float32)
    k[:, K_COS:K_COS + T] = np.cos(ang)
    k[:, K_SIN:K_SIN + T] = np.sin(ang)
    k[:, K_MASK:K_MASK + P] = np.where(np.arange(P)[None, :] <= np.arange(P)[:, None], 0.0, -1e30)
    k[:, K_OWN:K_OWN + NB * NB] = np.where(np.eye(NB) > 0, 0.0, -1e30).reshape(1, -1)
    for base in range(0, P, ROPE):
        for m in range(half):
            k[base + m + half, K_SWAP + base + m] = -1.0
            k[base + m, K_SWAP + base + m + half] = 1.0
    return k


def kernel(**inputs):
    import numpy as np
    import concourse.bacc as bacc
    from concourse.bass_utils import run_bass_kernel_spmd

    nc = bacc.Bacc("TRN2", target_bir_lowering=False, num_devices=1)
    arrays, ins, outs = {}, {}, {}
    for name in _INS:
        a = np.ascontiguousarray(inputs[name])
        arrays[f"in_{name}"] = a
        ins[name] = nc.dram_tensor(f"in_{name}", a.shape, mybir.dt.from_np(a.dtype), kind="ExternalInput").ap()
    arrays["in_consts"] = shape_constants()
    ins["consts"] = nc.dram_tensor("in_consts", (P, K_END), F32, kind="ExternalInput").ap()
    for name, shape in _OUTS.items():
        outs[name] = nc.dram_tensor(f"out_{name}", shape, F32, kind="ExternalOutput").ap()
    build(nc, ins, outs)
    r = run_bass_kernel_spmd(nc, [arrays], core_ids=[0])
    return tuple(r.results[0][f"out_{name}"] for name in _OUTS)
```

```python
from contextlib import ExitStack

import concourse.bass as bass
from concourse import mybir

F32 = mybir.dt.float32
F32R = mybir.dt.float32r
I32 = mybir.dt.int32
ALU = mybir.AluOpType
ACT = mybir.ActivationFunctionType
AX = mybir.AxisListType
ds = bass.ds

P = 128
D = 2048
KT = D // P
S = 256
NB = 8
T = S + NB
FF = 3 * D
FT = FF // P
SECTIONS = FF // D
H = 16
NOPE, ROPE, LORA = 128, 64, 512
LT = LORA // P
PAGES, PAGE = 8, 128
PHYS = (NB * PAGES * 5) // 4
KEYS = PAGES * PAGE + NB
ATTN_SCALE = 1.0 / float(NOPE + ROPE) ** 0.5
EPS = 1e-6
RG_C = 8.0
LG = 8

RAW, SPLIT = 8, 4
FFN_CHUNKS = SECTIONS * (64 + 32)
FFN_PAIRS = SECTIONS * (16 + 8)
C_RGX = 0
C_RGY = C_RGX + 32
C_RGO = C_RGY + 32
C_FFN0 = C_RGO + 32
C_DKV = C_FFN0 + FFN_CHUNKS
C_DQ = C_DKV + 12
C_UQ = C_DQ + 8
C_UK = C_UQ + 12
C_UV = C_UK + 8
C_MO = C_UV + 8
C_FFN1 = C_MO + 32
C_END = C_FFN1 + FFN_CHUNKS
G_RGX = 0
G_RGY = G_RGX + 8
G_RGO = G_RGY + 8
G_FFN0 = G_RGO + 8
G_DKV = G_FFN0 + FFN_PAIRS
G_DQ = G_DKV + 3
G_UQ = G_DQ + 2
G_UK = G_UQ + 12
G_UV = G_UK + 8
G_MO = G_UV + 8
G_FFN1 = G_MO + 8
G_END = G_FFN1 + FFN_PAIRS

RG_ROWS = 3 * NB + 4 + 1
GATE_ROWS = 3 + NB
FF_ROWS = 2 * NB + 3 + 1
PT_RG = 0
PT_GATE = PT_RG + RG_ROWS * KT
PT_FF = PT_GATE + GATE_ROWS * KT
PT_NORM = PT_FF + 2 * FF_ROWS * FT
PT_KVIN = PT_NORM + 8 * KT
PT_KVN = PT_KVIN + KT
PT_QN = PT_KVN + LT
PT_END = PT_QN + LT
PT_TILES = -(-PT_END // P)

K_ID = 0
K_COS = K_ID + P
K_SIN = K_COS + T
K_MASK = K_SIN + T
K_OWN = K_MASK + P
K_SWAP = K_OWN + NB * NB
K_END = K_SWAP + P

CS_FFN0 = 7 * KT
CS_FFN1 = CS_FFN0 + 5 * FT
H_FFN0 = KT
H_FFN1 = H_FFN0 + FT
XN_0, XN_1, XN_KV, XN_Q, XN_3 = (KT * n for n in range(5))
PAR_STEPS = 19
SQ_STEPS = 1 + 2 * (KT // 2 - 2)

N_X0, N_RGO, N_X1, N_F0, N_X2, N_C, N_CQ, N_MO, N_X3, N_F1 = range(10)


def parts(c):
    if C_DKV + 8 <= c < C_DQ:
        return 2
    if C_UQ <= c < C_UK:
        return 4 if (c - C_UQ) % 3 == 2 else 2
    return 1


def parts_before(c):
    return sum(parts(d) - 1 for d in range(C_DKV, min(c + 1, C_UK)) if d % RAW == c % RAW)


def loaded(c):
    return 16 * (c // RAW + 1 + parts_before(c))


class Semaphores:
    pass


def build(nc, I, O):
    with ExitStack() as ctx:
        def sem(name):
            return ctx.enter_context(nc.semaphore(name))

        at = [16512]

        def sb(name, shape, dt, offset=None):
            size = 4
            for n in shape[1:]:
                size *= n
            if offset is None:
                offset = at[0]
                at[0] += -(-size // 32) * 32
            assert offset + size <= 229344, (name, offset + size)
            return nc.alloc_sbuf_tensor_at(name, list(shape), dt, offset=offset)

        x = sb("x", [P, KT, T], F32)
        raw = sb("raw", [P, RAW, 4, 256], F32)
        hi = sb("hi", [P, SPLIT, 4, 256], F32R)
        lo = sb("lo", [P, SPLIT, 4, 256], F32R)
        pt_at = at[0]
        PT = sb("PT", [P, PT_END], F32)
        kc = sb("kc", [P, K_END], F32)
        ones = sb("ones", [P, P], F32)
        rx = sb("rx", [P, T], F32)
        rf = sb("rf", [P, T], F32)
        ssum = sb("ssum", [P, T], F32)
        rms = sb("rms", [P, T], F32)
        eps = sb("eps", [P, 1], F32)
        rg_at = at[0]
        rg_tail = sb("rg_tail", [P, KT, 3 + NB], F32)
        h_tail = sb("h_tail", [P, KT, 1 + NB], F32)
        ff_at = at[0]
        ff_tail = sb("ff_tail", [P, FT, 2 + NB], F32)
        xn_at = at[0]
        xnh = sb("xnh", [P, KT, T], F32R)
        xnl_at = at[0]
        xnl = sb("xnl", [P, KT, T], F32R)
        h_at = at[0]
        hh = sb("hh", [P, KT, T], F32R)
        hl = sb("hl", [P, KT, T], F32R)
        f_at = at[0]
        f = sb("f", [P, KT, T], F32)
        free_at = at[0]
        TILE2 = 2 * T * 4
        ptrows = sb("ptrows", [P, PT_TILES, P], F32, xn_at)
        xrows = sb("xrows", [P, 2, D], F32, f_at)
        xsrows = sb("xsrows", [NB, D], F32, free_at)
        soft = sb("soft", [P, 4, KT], F32, free_at + D * 4)
        sq_pair = sb("sq_pair", [P, 2, T], F32, xn_at)
        sq_sum = sb("sq_sum", [P, 2, T], F32, xn_at + 2 * T * 4)
        sq_last = sb("sq_last", [P, 2, T], F32, xn_at + 4 * T * 4)
        sq_h = sb("sq_h", [P, KT, T], F32, h_at)
        gs = sb("gs", [P, 2, T], F32, free_at)
        ge = sb("ge", [P, 2, T], F32, free_at + TILE2)
        cv = sb("cv", [P, 2, T], F32, free_at + 2 * TILE2)
        us = sb("us", [P, 2, T], F32, free_at + 3 * TILE2)
        cwf = sb("cwf", [P, FF_ROWS, 2], F32, free_at + 4 * TILE2)
        ta = sb("ta", [P, 2, T], F32, free_at + 2 * TILE2)
        ti = sb("ti", [P, 2, T], F32, free_at + 3 * TILE2)
        r1 = sb("r1", [P, 2, T], F32, free_at + 4 * TILE2)
        aa = sb("aa", [P, 2, T], F32, free_at + 5 * TILE2)
        sq = sb("sq", [P, 2, T], F32, free_at + 6 * TILE2)
        gw_at = free_at + 7 * TILE2
        gw = sb("gw", [P, 2, 4, 256], F32, gw_at)
        cwr = sb("cwr", [P, RG_ROWS, 2], F32, ff_at)
        gp = sb("gp", [P, GATE_ROWS, 2], F32, ff_at + 256)
        cT = sb("cT", [P, LT, T], F32, free_at)
        cTh = sb("cTh", [P, LT, T], F32R, free_at + 2 * TILE2)
        cTl = sb("cTl", [P, LT, T], F32R, free_at + 4 * TILE2)
        krT = sb("krT", [P, T], F32, free_at + 6 * TILE2)
        mla_at = free_at + 6 * TILE2 + T * 4
        cqh = sb("cqh", [P, LT, T], F32R, mla_at)
        cql = sb("cql", [P, LT, T], F32R, mla_at + 2 * TILE2)
        pre = sb("pre", [P, LT, T], F32, f_at)
        prk = sb("prk", [P, T], F32, f_at + 2 * TILE2)
        sqs = sb("sqs", [P, LT, T], F32, f_at + 3 * TILE2)
        preq = sb("preq", [P, LT, T], F32, f_at + 5 * TILE2)
        rot = sb("rot", [P, 2, T], F32, f_at + 7 * TILE2)
        qn = sb("qn", [P, H, T], F32, xn_at)
        qr = sb("qr", [P, H // 2, T], F32, xnl_at)
        mid_at = xnl_at + 4 * TILE2
        ukTh = sb("ukTh", [P, 4, LORA], F32R, h_at + 16 * LORA * 2)
        ukTl = sb("ukTl", [P, 4, LORA], F32R, h_at + 24 * LORA * 2)
        qsh = sb("qsh", [P, H, NB], F32R, mid_at + 2048)
        qsl = sb("qsl", [P, H, NB], F32R, mid_at + 2560)
        olh = sb("olh", [P, LT, H, NB], F32R, mid_at + 4096)
        oll = sb("oll", [P, LT, H, NB], F32R, mid_at)
        qlat = sb("qlat", [P, LT, NB, H], F32, mid_at)
        olat = sb("olat", [P, LT, H, NB], F32, mid_at + 2048)
        cnew = sb("cnew", [NB, LORA], F32, mid_at + 4096)
        qrs = sb("qrs", [ROPE, NB, H], F32, mid_at + 6144)
        qb = sb("qb", [P, LT, H], F32, mid_at + 6656)
        qrb = sb("qrb", [ROPE, H], F32, mid_at + 6912)
        ptab = sb("ptab", [1, NB * PAGES], I32, mid_at + 7168)
        stats = sb("stats", [P, 16], F32, mid_at + 6976)
        kn = sb("kn", [P, H, S], F32, f_at)
        cpage = sb("cpage", [P, 4, 4, LORA], F32, h_at)
        kpage = sb("kpage", [P, 4, 4, ROPE], F32, mla_at)
        ctp = sb("ctp", [P, 2, LT, P], F32, mla_at + 4096)
        krp = sb("krp", [ROPE, 2, P], F32, mla_at + 8192)
        sp_ = sb("sp_", [H, KEYS], F32, pt_at)
        sout = sb("sout", [H, LORA], F32, pt_at + KEYS * 4)
        assert KEYS + LORA <= PT_FF + FF_ROWS * FT
        spT = sb("spT", [P, PAGES + 1, H], F32, rg_at)
        Vs = sb("Vs", [P, 2, 2, 256], F32, mla_at)
        sm = sb("sm", [P, 2, 3 * P], F32, mla_at + 4096)
        pTs = sb("pTs", [P, 2, 3 * P], F32, pt_at)
        rows = sb("rows", [P, 4, 512], F32, h_at)
        yrows = sb("yrows", [P, 4, 512], F32, h_at)

        acc = [ctx.enter_context(nc.psum_tensor(f"acc{n}", [P, 512], F32)) for n in range(4)]
        mis = [ctx.enter_context(nc.psum_tensor(f"mis{n}", [P, 512], F32)) for n in range(4)]

        pT_ps, o_ps = (mis[2], acc[1]), (acc[3], mis[3])

        ident = kc[:, K_ID:K_ID + P]
        cos_ = kc[:, K_COS:K_COS + T]
        sin_ = kc[:, K_SIN:K_SIN + T]
        mask = kc[:, K_MASK:K_MASK + P]
        swap = kc[:, K_SWAP:K_SWAP + P]

        def gain(l, n, j):
            c = PT_NORM + (l * 4 + n) * KT + j
            return PT[:, c:c + 1]

        def pcol(base, j):
            return PT[:, base + j:base + j + 1]

        s = Semaphores()
        s.hi_ready = sem("hi_ready")
        s.lo_ready = sem("lo_ready")
        s.chunk_used = sem("chunk_used")
        s.acc_read = sem("acc_read")
        s.const_in = sem("const_in")
        s.rows_in = [sem(f"rows_in{n}") for n in range(2)]
        s.x_in = sem("x_in")
        s.ones_set = sem("ones_set")
        s.turned = sem("turned")
        s.pt_ready = sem("pt_ready")
        s.x_turned = sem("x_turned")
        s.par_step = sem("par_step")
        s.sq_done = sem("sq_done")
        s.sum_ready = sem("sum_ready")
        s.stat_ready = sem("stat_ready")
        s.rms_ready = sem("rms_ready")
        s.sq_step = sem("sq_step")
        s.sum_step = sem("sum_step")
        s.rstd_ready = sem("rstd_ready")
        s.fnorm = sem("fnorm")
        s.x_tile = sem("x_tile")
        s.xn_hi = sem("xn_hi")
        s.xn_ready = sem("xn_ready")
        s.cw_ready = sem("cw_ready")
        s.conv_step = sem("conv_step")
        s.tail_saved = sem("tail_saved")
        s.gelu_done = sem("gelu_done")
        s.h_full = sem("h_full")
        s.h_hi = sem("h_hi")
        s.h_ready = sem("h_ready")
        s.gates = sem("gates")
        s.gate_par = sem("gate_par")
        s.gate_tanh = sem("gate_tanh")
        s.gate_th = sem("gate_th")
        s.gate_step = sem("gate_step")
        s.ht_saved = sem("ht_saved")
        s.decay = sem("decay")
        s.c_step = sem("c_step")
        s.c_hi = sem("c_hi")
        s.c_ready = sem("c_ready")
        s.kr_rot = sem("kr_rot")
        s.kr_step = sem("kr_step")
        s.q_rot = sem("q_rot")
        s.q_step = sem("q_step")
        s.uk_turned = sem("uk_turned")
        s.uk_hi = sem("uk_hi")
        s.uk_read = sem("uk_read")
        s.qs_hi = sem("qs_hi")
        s.qs_ready = sem("qs_ready")
        s.ql_done = sem("ql_done")
        s.ql_ready = sem("ql_ready")
        s.sh_done = sem("sh_done")
        s.sh_ready = sem("sh_ready")
        s.cn_turned = sem("cn_turned")
        s.cn_ready = sem("cn_ready")
        s.ptab_in = sem("ptab_in")
        s.pg_turned = sem("pg_turned")
        s.pg_c = sem("pg_c")
        s.pg_k = sem("pg_k")
        s.qb_ready = sem("qb_ready")
        s.s_scored = sem("s_scored")
        s.s_step = sem("s_step")
        s.s_exp = sem("s_exp")
        s.s_norm = sem("s_norm")
        s.so_turned = sem("so_turned")
        s.s_turned = sem("s_turned")
        s.s_pT = sem("s_pT")
        s.s_out = sem("s_out")
        s.ol_ready = sem("ol_ready")
        s.scored = sem("scored")
        s.sm_step = sem("sm_step")
        s.sm_exp = sem("sm_exp")
        s.prob = sem("prob")
        s.p_turned = sem("p_turned")
        s.pT_ready = sem("pT_ready")
        s.o_ps = sem("o_ps")
        s.ol_hi = sem("ol_hi")
        s.ol_split = sem("ol_split")
        s.o_hi = sem("o_hi")
        s.o_ready = sem("o_ready")
        s.out_turned = sem("out_turned")
        s.out_rows = sem("out_rows")
        s.shifted = sem("shifted")
        s.raw_loaded = [sem(f"raw_loaded{n}") for n in range(RAW)]
        s.gw_loaded = [sem(f"gw_loaded{n}") for n in range(2)]
        s.page_in = [sem(f"page_in{n}") for n in range(4)]
        s.mid_sent = [sem(f"mid_sent{n}") for n in range(4)]
        s.end_sent = [sem(f"end_sent{n}") for n in range(4)]
        block = ctx.enter_context(nc.Block())

        def out_plan_mid():
            for g in range(KT // 4):
                yield [rg_tail[:, 4 * g + k, :] for k in range(4)], 3 + NB, [
                    (O["p_rgc"][0, 0, :, 512 * g:512 * g + 512], 0, 3),
                    (O["s_rgc"][0, :, 2, 512 * g:512 * g + 512], 3, NB)]
            for g in range(KT // 4):
                yield [h_tail[:, 4 * g + k, :] for k in range(4)], 1 + NB, [
                    (O["p_h"][0, :, 512 * g:512 * g + 512], 0, 1),
                    (O["s_h"][0, :, 512 * g:512 * g + 512], 1, NB)]
            yield from out_plan_ff(0)

        def out_plan_ff(l):
            for g in range(FT // 4):
                yield [ff_tail[:, 4 * g + k, :] for k in range(4)], 2 + NB, [
                    (O["p_ffc"][l, 0, :, 512 * g:512 * g + 512], 0, 2),
                    (O["s_ffc"][l, :, 1, 512 * g:512 * g + 512], 2, NB)]

        def out_plan_c():
            for t in range(2):
                yield [cT[:, k, t * P:(t + 1) * P] for k in range(LT)], P, [
                    (O["p_kv"][0, t * P:(t + 1) * P, :], 0, P)]
            yield [cT[:, k, S:T] for k in range(LT)], NB, [(O["s_kv"][:, 0, :], 0, NB)]
            for t in range(2):
                yield [krT[0:ROPE, t * P:(t + 1) * P]], P, [(O["p_kr"][0, t * P:(t + 1) * P, :], 0, P)]
            yield [krT[0:ROPE, S:T]], NB, [(O["s_kr"][:, 0, :], 0, NB)]

        def out_plan_y():
            for g in range(KT // 4):
                for t in range(2):
                    yield [x[:, 4 * g + k, t * P:(t + 1) * P] for k in range(4)], P, [
                        (O["y_p"][0, t * P:(t + 1) * P, 512 * g:512 * g + 512], 0, P)]
                yield [x[:, 4 * g + k, S:T] for k in range(4)], NB, [
                    (O["y_s"][:, 0, 512 * g:512 * g + 512], 0, NB)]

        mid = list(out_plan_mid()) + list(out_plan_c())
        end = list(out_plan_ff(1)) + list(out_plan_y())
        plan = mid + end

        def sent(n):
            first = 0 if n < len(mid) else len(mid)
            sems = s.end_sent if first else s.mid_sent
            k = (n - first) % 4
            return sems[k], sum(16 * len(plan[m][2]) for m in range(first + k, n + 1, 4))

        def row_slot(n):
            return rows[:, n % 4, :] if n < len(mid) else yrows[:, (n - len(mid)) % 4, :]

        def row_width(tiles):
            return sum(t.shape[0] for t in tiles)

        def send(engine, n):
            engine.wait_ge(s.out_rows, n + 1)
            for dst, r, m in plan[n][2]:
                engine.dma_start(dst, row_slot(n)[r:r + m, 0:row_width(plan[n][0])]).then_inc(sent(n)[0], 16)

        def row_bank(n):
            return mis[n % 2] if n < len(mid) else mis[(n - len(mid)) % 3]

        row_plan = []
        row_plan += [
            (PT_RG, I["state_rglru_conv"].rearrange("a b k (j p) -> (a b k j) p", p=P)),
            (PT_RG + 3 * NB * KT, I["conv_rg_w"].rearrange("a k (j p) -> (a k j) p", p=P)),
            (PT_RG + (3 * NB + 4) * KT, I["conv_rg_b"].rearrange("a (j p) -> (a j) p", p=P)),
            (PT_GATE, I["b_rg_a"].rearrange("a (j p) -> (a j) p", p=P)),
            (PT_GATE + KT, I["b_rg_i"].rearrange("a (j p) -> (a j) p", p=P)),
            (PT_GATE + 2 * KT, I["rg_lambda"].rearrange("a (j p) -> (a j) p", p=P)),
            (PT_GATE + 3 * KT, I["state_rglru_h"].rearrange("a b (j p) -> (a b j) p", p=P)),
            (PT_NORM, I["norm_g"].rearrange("l n (j p) -> (l n j) p", p=P)),
            (PT_KVIN, I["kv_in_g"].rearrange("(j p) -> j p", p=P)),
            (PT_KVN, I["kv_norm_g"].rearrange("(j p) -> j p", p=P)),
            (PT_QN, I["q_norm_g"].rearrange("a (j p) -> (a j) p", p=P)),
        ]
        for l in range(2):
            base = PT_FF + l * FF_ROWS * FT
            row_plan += [
                (base, I["state_ffn_conv"][l].rearrange("b k (j p) -> (b k j) p", p=P)),
                (base + 2 * NB * FT, I["ffn_conv_w"][l].rearrange("k (j p) -> (k j) p", p=P)),
                (base + (2 * NB + 3) * FT, I["ffn_conv_b"][l:l + 1].rearrange("a (j p) -> (a j) p", p=P)),
            ]
        row_pieces = []
        for base, src in row_plan:
            r = 0
            while r < src.shape[0]:
                t, q = divmod(base + r, P)
                m = min(src.shape[0] - r, P - q)
                row_pieces.append((q, t, src[r:r + m, :]))
                r += m

        @block.sync
        def _(sp):
            def chunk(c, src, dst=None, off=0, part=0):
                if part == 0 and c >= RAW:
                    sp.wait_ge(s.lo_ready, off + (c - RAW + 1))
                if part == 0 and C_UK <= c - RAW < C_UV:
                    sp.wait_ge(s.chunk_used, off + (c - RAW + 1))
                dst = raw[:, c % RAW, :, :] if dst is None else dst
                sp.dma_start(dst, src).then_inc(s.raw_loaded[c % RAW], 16)

            def rows4(w, q, col, n=256):
                return w[512 * q:512 * q + 512, ds(col, n)].rearrange("(k p) n -> p k n", p=P)

            def stream(w, c0, col0, pairs):
                with sp.Fori(0, pairs // 2) as i:
                    for a in range(2):
                        for q in range(4):
                            chunk(c0 + 4 * a + q, rows4(w, q, i * 512 + (col0 + 256 * a)), off=i * 8)

            def ffn(l, c0):
                with sp.Fori(0, SECTIONS) as sec:
                    with sp.Fori(0, 8) as i:
                        for a, w in enumerate((I["w_ffn_g"], I["w_ffn_u"])):
                            for q in range(4):
                                chunk(c0 + 4 * a + q, rows4(w[l], q, sec * D + i * 256),
                                      off=sec * 96 + i * 8)
                    with sp.Fori(0, 4) as i:
                        for a in range(2):
                            for q in range(4):
                                w = I["w_ffn_d"][l][ds(sec * D + 512 * q, 512), ds(i * 512 + 256 * a, 256)]
                                chunk(c0 + 64 + 4 * a + q, w.rearrange("(k p) n -> p k n", p=P),
                                      off=sec * 96 + i * 8)

            for n, (q, t, src) in enumerate(row_pieces):
                if n % 4:
                    sp.dma_start(ptrows[q:q + src.shape[0], t, :], src).then_inc(s.rows_in[0], 16)
            sp.wait_ge(s.x_in, 32)
            for a in range(2):
                for q in range(4):
                    chunk(C_RGX + 4 * a + q, rows4(I["w_rg_in"][0], q, 256 * a))
            stream(I["w_rg_in"][0], C_RGX + 8, 512, 6)
            stream(I["w_rg_in"][0], C_RGY, D, 8)
            stream(I["w_rg_o"][0], C_RGO, 0, 8)
            ffn(0, C_FFN0)
            for a in range(2):
                for q in range(4):
                    chunk(C_DKV + 4 * a + q, rows4(I["w_dkv"], q, 256 * a))
            for q in range(4):
                for e in range(2):
                    c = C_DKV + 8 + q
                    chunk(c, rows4(I["w_dkv"], q, LORA, ROPE),
                          raw[:, c % RAW, :, ROPE * e:ROPE * e + ROPE], part=e)
            for a in range(2):
                for q in range(4):
                    chunk(C_DQ + 4 * a + q, rows4(I["w_dq"][0], q, 256 * a))
            for g in range(4):
                for e in range(3):
                    c = C_UQ + 3 * g + e
                    for m in range(parts(c)):
                        if e < 2:
                            src = I["w_uq"][0, :, 4 * g + 2 * e + m, 0:NOPE]
                            dst = raw[:, c % RAW, :, NOPE * m:NOPE * (m + 1)]
                        else:
                            src = I["w_uq"][0, :, 4 * g + m, NOPE:NOPE + ROPE]
                            dst = raw[:, c % RAW, :, ROPE * m:ROPE * (m + 1)]
                        chunk(c, src.rearrange("(k p) n -> p k n", p=P), dst, part=m)
            for u in range(8):
                chunk(C_UK + u, rows4(I["w_uk"].rearrange("c h d -> c (h d)"), 0, 256 * u))
            for u in range(8):
                chunk(C_UV + u, rows4(I["w_uv"].rearrange("c h d -> c (h d)"), 0, 256 * u))
            sp.wait_ge(s.ptab_in, 16)
            sp.wait_ge(s.chunk_used, C_UK)
            for n in range(len(mid) - 4, len(mid)):
                sp.wait_ge(*sent(n))
            kcache = I["cache_k_rope"]
            ccache = I["cache_kv_latent"]

            def half(i, n, first):
                if not first:
                    sp.wait_ge(s.s_out, i * 2 + (n // 2 - 1))
                for g in range(4):
                    page = sp.value_load(ptab[0:1, ds(i * 16 + (4 * n + g), 1)], min_val=0, max_val=PHYS - 1)
                    sp.dma_start(cpage[:, n, g, :], ccache[ds(page, 1), :, :].rearrange("a k c -> k (a c)"))\
                        .then_inc(s.page_in[n], 16)
                    sp.dma_start(kpage[:, n, g, :], kcache[ds(page, 1), :, :].rearrange("a k c -> k (a c)"))\
                        .then_inc(s.page_in[n], 16)

            for n in range(4):
                if n == 2:
                    sp.wait_ge(s.ql_done, H)
                half(0, n, True)
            with sp.Fori(1, NB // 2) as i:
                for n in range(4):
                    half(i, n, False)
            for a in range(2):
                for q in range(4):
                    chunk(C_MO + 4 * a + q, rows4(I["w_mla_o"][0], q, 256 * a))
            stream(I["w_mla_o"][0], C_MO + 8, 512, 6)
            ffn(1, C_FFN1)
            for n in range(len(mid), len(plan)):
                send(sp, n)
            for n in range(len(plan) - 4, len(plan)):
                sp.wait_ge(*sent(n))

        MID_BEFORE, MID_STALL = 3, 8

        def mid_with(e):
            rest = len(mid) - MID_STALL
            return range(MID_STALL + rest * e // 12, MID_STALL + rest * (e + 1) // 12)

        @block.gpsimd
        def _(pool):
            for q, t, src in row_pieces[0::4]:
                pool.dma_start(ptrows[q:q + src.shape[0], t, :], src).then_inc(s.rows_in[1], 16)
            pool.dma_start(O["s_rgc"][0, :, 0:2, :], I["state_rglru_conv"][0, :, 1:3, :]).then_inc(s.shifted, 16)
            pool.dma_start(O["s_ffc"][:, :, 0, :].rearrange("l b f -> (l b) f"),
                           I["state_ffn_conv"][:, :, 1, :].rearrange("l b f -> (l b) f")).then_inc(s.shifted, 16)

            def columns(dst, base, nrows, tiles, first):
                src = PT[:, base:base + nrows * tiles].rearrange("p (r j) -> p r j", j=tiles)
                return pool.tensor_copy(dst, src[:, :, ds(first, 2)])

            def gate_weights(i, a):
                for e, w in enumerate((I["w_rg_a"], I["w_rg_i"])):
                    src = w[0, ds(i * 2 + a, 1), :, :].rearrange("h (k p) n -> p (h k) n", p=P)
                    pool.dma_start(gw[:, a, 2 * e:2 * e + 2, :], src).then_inc(s.gw_loaded[a], 16)

            def gate_pairs(i, more):
                for a in range(2):
                    columns(gp[:, :, :], PT_GATE, GATE_ROWS, KT, i * 4 + 2 * a).then_inc(s.gate_par, 1)
                    pool.wait_ge(s.gate_step, i * 16 + (8 * a + 2))
                    pool.tensor_tensor(aa[:, :, :], ta[:, :, :], r1[:, :, :], ALU.mult).then_inc(s.decay, 1)
                    pool.wait_ge(s.decay, i * 6 + (3 * a + 1))
                    pool.tensor_tensor(aa[:, :, :], r1[:, :, :], aa[:, :, :], ALU.subtract).then_inc(s.decay, 1)
                    pool.wait_ge(s.decay, i * 6 + (3 * a + 2))
                    h0 = gp[:, 3:3 + NB, :].rearrange("p b m -> p m b")
                    pool.tensor_tensor(aa[:, :, S:T], aa[:, :, S:T], h0, ALU.mult).then_inc(s.decay, 1)
                    pool.wait_ge(s.gate_step, i * 16 + (8 * a + 8))
                    pool.tensor_copy(h_tail[:, ds(i * 4 + 2 * a, 2), :],
                                     f[:, ds(i * 4 + 2 * a, 2), S - 1:T]).then_inc(s.ht_saved, 1)
                    if more:
                        gate_weights(i + 1, a)

            pool.wait_ge(s.pt_ready, 6)
            for a in range(2):
                gate_weights(0, a)
            with pool.Fori(0, 8) as i:
                columns(cwr[:, :, :], PT_RG, RG_ROWS, KT, i * 2).then_inc(s.cw_ready, 1)
                pool.wait_ge(s.acc_read, i * 2 + 2)
                pool.tensor_copy(rg_tail[:, ds(i * 2, 2), :], gs[:, :, S - 3:T]).then_inc(s.tail_saved, 1)
                pool.wait_ge(s.conv_step, i * 14 + 14)
            pool.wait_ge(s.par_step, PAR_STEPS)
            with pool.Fori(0, 3) as i:
                gate_pairs(i, True)
            gate_pairs(3, False)

            def squares(b, g0):
                done = SQ_STEPS * b
                for j in range(KT // 2 - 1):
                    pool.wait_ge(s.acc_read, 2 * (g0 + j + 1))
                    tiles = f[:, 2 * j:2 * j + 2, :]
                    if j == 0:
                        pool.tensor_tensor(sq_sum[:, :, :], tiles, tiles, ALU.mult).then_inc(s.sq_step, 1)
                        continue
                    if j >= 2:
                        pool.wait_ge(s.sq_step, done + 2 * j - 1)
                    pool.tensor_tensor(sq_pair[:, :, :], tiles, tiles, ALU.mult).then_inc(s.sq_step, 1)
                    pool.wait_ge(s.sq_step, done + 2 * j)
                    pool.tensor_tensor(sq_sum[:, :, :], sq_sum[:, :, :], sq_pair[:, :, :], ALU.add)\
                        .then_inc(s.sq_step, 1)
                for j in range(KT):
                    pool.wait_ge(s.fnorm, 16 * b + j + 1)
                    pool.tensor_tensor(x[:, j, :], x[:, j, :], f[:, j, :], ALU.add).then_inc(s.x_tile, 1)

            def ffn(l, cs0, cw0):
                with pool.Fori(0, SECTIONS) as sec:
                    with pool.Fori(0, 8) as i:
                        pool.wait_ge(s.conv_step, sec * 80 + i * 10 + cs0)
                        columns(cwf[:, :, :], PT_FF + l * FF_ROWS * FT, FF_ROWS, FT, sec * 16 + i * 2)\
                            .then_inc(s.cw_ready, 1)
                        g = G_FFN0 if l == 0 else G_FFN1
                        pool.wait_ge(s.acc_read, sec * 48 + i * 4 + (2 * g + 2))
                        pool.tensor_copy(ff_tail[:, ds(sec * 16 + i * 2, 2), :], gs[:, :, S - 2:T])\
                            .then_inc(s.tail_saved, 1)

            squares(0, G_RGO)
            ffn(0, CS_FFN0, 8)
            squares(1, G_DKV - KT // 2)
            pool.wait_ge(s.chunk_used, C_DQ)
            pool.dma_start(ptab[0:1, :], I["page_table"].rearrange("(a b) n -> a (b n)", a=1)).then_inc(s.ptab_in, 16)
            for n in range(len(mid)):
                send(pool, n)
            squares(2, G_MO)
            ffn(1, CS_FFN1, 32)
            squares(3, G_END - KT // 2)
            pool.wait_ge(s.shifted, 32)

        def split_width(c):
            return P if C_DKV + 8 <= c < C_DQ else 256

        @block.scalar
        def _(act):
            def split(c, off=0):
                act.wait_ge(s.raw_loaded[c % RAW], (off * 2) + loaded(c))
                if c >= SPLIT:
                    act.wait_ge(s.chunk_used, off + (c - SPLIT + 1))
                n = split_width(c)
                act.activation(hi[:, c % SPLIT, :, 0:n], raw[:, c % RAW, :, 0:n], ACT.Copy).then_inc(s.hi_ready, 1)

            def high_pair(src, done, tile):
                for m in range(2):
                    act.wait_ge(s.h_full, done + (m + 1))
                    act.activation(hh[:, ds(tile + m, 1), :], src[:, m:m + 1, :], ACT.Copy).then_inc(s.h_hi, 1)

            def norm(src, sq_to, tiles):
                act.activation(sq_to[:, 0:tiles, :], src[:, 0:tiles, :], ACT.Square).then_inc(s.sq_done, 1)

            def root(n, features):
                act.wait_ge(s.stat_ready, n + 1)
                if n:
                    act.wait_ge(s.rstd_ready, n)
                act.activation(rms[:, :], mis[3][:, 0:T], ACT.Sqrt, scale=1.0 / features, bias=eps[:, 0:1])\
                    .then_inc(s.rms_ready, 1)

            def scaled(dst, base, xt):
                for j in range(KT):
                    act.wait_ge(s.x_tile, xt + j + 1)
                    act.activation(dst[:, j, :], x[:, j, :], ACT.Copy, scale=PT[:, base + j:base + j + 1])\
                        .then_inc(s.xn_hi, 1)

            def ramp(n, base, xt, sq_to, c0):
                for j in range(KT):
                    act.wait_ge(s.x_tile, xt + j + 1)
                    act.activation(xnh[:, j, :], x[:, j, :], ACT.Copy, scale=PT[:, base + j:base + j + 1])\
                        .then_inc(s.xn_hi, 1)
                    last = act.activation(sq_to[:, j, :], x[:, j, :], ACT.Square)
                    if j == 11:
                        split(c0 + 4)
                    if j == 15:
                        split(c0 + 5)
                last.then_inc(s.sq_done, 1)
                split(c0 + 6)
                split(c0 + 7)

            act.dma_start(kc[:, :], I["consts"]).then_inc(s.const_in, 16)
            act.dma_start(xrows[:, :, :], I["x_prompt"][0].rearrange("(t p) d -> p t d", p=P)).then_inc(s.x_in, 16)
            act.dma_start(xsrows[:, :], I["x_sample"][:, 0, :]).then_inc(s.x_in, 16)
            for n in range(6):
                act.wait_ge(s.turned, n + 1)
                w = min(512, PT_END - 512 * n)
                act.activation(PT[:, 512 * n:512 * n + w], mis[n % 4][:, 0:w], ACT.Copy).then_inc(s.pt_ready, 1)
            act.wait_ge(s.pt_ready, 6)
            for c in range(4):
                split(c)
            ramp(N_X0, PT_NORM, 0, sq_h, C_RGX)
            root(N_X0, D)
            act.activation(soft[:, 0, :], PT[:, PT_GATE + 2 * KT:PT_GATE + 3 * KT], ACT.Abs).then_inc(s.par_step, 1)
            act.wait_ge(s.par_step, 1)
            act.activation(soft[:, 1, :], soft[:, 0, :], ACT.Exp, scale=-1.0).then_inc(s.par_step, 1)
            for c in range(8, 12):
                split(C_RGX + c)
            with act.Fori(1, 4) as i:
                for c in range(8):
                    split(C_RGX + 4 + c, off=i * 8)
            def gate_tanhs(i, b):
                act.wait_ge(s.gates, i * 2 + (b + 1))
                act.wait_ge(s.gate_par, i * 2 + (b + 1))
                if b:
                    act.wait_ge(s.gate_step, i * 16 + 8 * b)
                for m in range(2):
                    act.activation(ta[:, m, :], mis[m][:, 0:T], ACT.Tanh, scale=0.5, bias=gp[:, 0, m:m + 1])\
                        .then_inc(s.gate_tanh, 1)
                for m in range(2):
                    act.activation(ti[:, m, :], mis[2 + m][:, 0:T], ACT.Tanh, scale=0.5,
                                   bias=gp[:, 1, m:m + 1]).then_inc(s.gate_tanh, 1)
                for m in range(2):
                    act.wait_ge(s.gate_tanh, i * 8 + (4 * b + m + 1))
                    act.activation(ta[:, m, :], ta[:, m, :], ACT.Tanh, scale=gp[:, 2, m:m + 1],
                                   bias=gp[:, 2, m:m + 1]).then_inc(s.gate_th, 1)
                act.wait_ge(s.gate_th, i * 6 + (3 * b + 2))
                act.activation(sq[:, :, :], ta[:, :, :], ACT.Sqrt).then_inc(s.gate_th, 1)

            def gelu_pair(i, a, following=True):
                if following:
                    gate_tanhs(i, a + 1)
                for c in range(4):
                    split(C_RGY + 4 + 4 * a + c, off=i * 8)
                for m in range(2):
                    act.wait_ge(s.acc_read, i * 4 + (2 * a + 2 * G_RGY + m + 1))
                    act.activation(ge[:, m, :], gs[:, m, :], ACT.Gelu_apprx_tanh).then_inc(s.gelu_done, 1)
                high_pair(ge, i * 4 + 2 * a, i * 4 + 2 * a)
                act.wait_ge(s.h_ready, i * 4 + (2 * a + 2))

            gate_tanhs(0, 0)
            with act.Fori(0, 3) as i:
                for a in range(2):
                    gelu_pair(i, a)
            gelu_pair(3, 0)
            gelu_pair(3, 1, following=False)
            with act.Fori(0, 4) as i:
                for c in range(8):
                    split(C_RGO + 4 + c, off=i * 8)

            def block_norm(b, n_f, acc_done, rows_first=()):
                act.wait_ge(s.acc_read, acc_done)
                norm(f[:, KT - 2:KT, :], sq_last, 2)
                for n in rows_first:
                    rows_out(n)
                root(n_f, D)

            def section(l, c0, h0, sec):
                def pair(i, lead=True):
                    if lead:
                        for c in range(4):
                            split(c0 + 4 + c, off=i * 8)
                    act.wait_ge(s.conv_step, i * 10 + (80 * sec + (CS_FFN0, CS_FFN1)[l] + 10))
                    for m in range(2):
                        act.activation(ge[:, m, :], cv[:, m, :], ACT.Gelu_apprx_tanh).then_inc(s.gelu_done, 1)
                    for c in range(4):
                        split(c0 + 8 + c, off=i * 8)
                    high_pair(us, i * 2 + (16 * sec + h0), i * 2)

                if sec == 0:
                    pair(0, lead=False)
                with act.Fori(1 if sec == 0 else 0, 8) as i:
                    pair(i)
                last = sec == SECTIONS - 1 and l == 1
                with act.Fori(0, 3 if last else 4) as i:
                    for c in range(8):
                        split(c0 + 68 + c, off=i * 8)
                if last:
                    for c in range(4):
                        split(c0 + 92 + c)

            def ffn(l, c0, h0):
                for sec in range(SECTIONS):
                    section(l, c0 + 96 * sec, h0, sec)

            block_norm(0, N_RGO, 2 * G_FFN0)
            ramp(N_X1, PT_NORM + 2 * KT, 16, f, C_FFN0)
            root(N_X1, D)
            ffn(0, C_FFN0, H_FFN0)
            block_norm(1, N_F0, 2 * G_DKV)
            ramp(N_X2, PT_KVIN, 32, f, C_DKV)
            scaled(hh, PT_NORM + 4 * KT, 32)
            root(N_X2, D)
            for c in range(C_DKV + 8, C_DKV + 16):
                split(c)
            act.wait_ge(s.acc_read, 2 * G_DKV + 4)
            norm(pre, sqs, LT)
            for c in range(C_DQ + 4, C_DQ + 8):
                split(c)
            root(N_C, LORA)
            for c in range(C_DQ + 8, C_DQ + 12):
                split(c)
            act.wait_ge(s.c_step, LT)
            act.activation(cTh[:, :, :], cT[:, :, :], ACT.Copy).then_inc(s.c_hi, 1)
            def rows_out(n):
                act.wait_ge(s.out_turned, n + 1)
                if 4 <= n < len(mid) or n >= len(mid) + 4:
                    act.wait_ge(*sent(n - 4))
                tiles, m, _ = plan[n]
                w = row_width(tiles)
                act.activation(row_slot(n)[0:m, 0:w], row_bank(n)[0:m, 0:w], ACT.Copy).then_inc(s.out_rows, 1)

            act.wait_ge(s.acc_read, 2 * G_UQ)
            norm(preq, sqs, LT)
            for n in range(MID_BEFORE):
                rows_out(n)
            root(N_CQ, LORA)
            for n in range(MID_BEFORE, MID_STALL):
                rows_out(n)
            act.wait_ge(s.c_step, 2 * LT)
            act.activation(cqh[:, :, :], preq[:, :, :], ACT.Copy).then_inc(s.c_hi, 1)
            for e in range(12):
                split(C_UQ + 4 + e)
                for n in mid_with(e):
                    rows_out(n)
            act.wait_ge(s.cn_turned, 1)
            act.activation(cnew[:, :], mis[0][0:NB, :], ACT.Copy).then_inc(s.cn_ready, 1)
            act.wait_ge(s.sh_done, 1)
            shifted = mis[1][0:ROPE, 0:NB * H // 2].rearrange("p (g b) -> p b g", b=NB)
            heads = qrs[:, :, :].rearrange("p b (g e) -> p b g e", e=2)
            act.activation(heads[:, :, :, 1], shifted, ACT.Copy).then_inc(s.sh_ready, 1)
            act.activation(heads[:, :, :, 0], qr[0:ROPE, :, S:T].rearrange("p g b -> p b g"), ACT.Copy)\
                .then_inc(s.sh_ready, 1)
            act.activation(qsh[:, :, :], qn[:, :, S:T], ACT.Copy).then_inc(s.qs_hi, 1)

            def latent_queries(u):
                for m in range(2):
                    h = 2 * u + m
                    act.wait_ge(s.ql_done, h + 1)
                    src = mis[2 + m][:, 0:LT * NB].rearrange("p (c b) -> p c b", b=NB)
                    act.activation(qlat[:, :, :, h], src, ACT.Copy).then_inc(s.ql_ready, 1)

            for u in range(8):
                split(C_UK + 4 + u)
                for m in range(2):
                    h = 2 * u + m
                    act.wait_ge(s.uk_turned, h + 1)
                    if u >= 2:
                        act.wait_ge(s.ql_done, h - 3)
                    act.activation(ukTh[:, h % 4, :], mis[m][:, :], ACT.Copy).then_inc(s.uk_hi, 1)
                if u:
                    latent_queries(u - 1)
            latent_queries(7)
            act.wait_ge(s.ql_ready, H)
            act.wait_ge(s.sh_ready, 2)
            def sample_step(i, b, pages, post):
                if pages:
                    if b:
                        act.wait_ge(s.s_scored, i * 2 + b)
                    act.activation(qb[:, :, :], qlat[:, :, ds(i * 2 + b, 1), :].rearrange("p c a h -> p c (a h)"),
                                   ACT.Copy).then_inc(s.qb_ready, 1)
                    act.activation(qrb[:, :], qrs[:, ds(i * 2 + b, 1), :].rearrange("p a h -> p (a h)"),
                                   ACT.Copy).then_inc(s.qb_ready, 1)
                for g in range(PAGES):
                    if pages:
                        act.wait_ge(s.pg_turned, i * 16 + (8 * b + g + 1))
                        act.activation(ctp[:, g % 2, :, :].rearrange("p c k -> p (c k)"), acc[g % 2][:, :],
                                       ACT.Copy).then_inc(s.pg_c, 1)
                    if post and g == 1:
                        act.wait_ge(s.s_step, i * 12 + (6 * b - 1))
                        act.activation(sp_[:, :], sp_[:, :], ACT.Exp, scale=ATTN_SCALE, bias=stats[0:H, 1:2],
                                       accum_out=stats[0:H, 2:3]).then_inc(s.s_exp, 1)
                    if post and g == 3:
                        act.wait_ge(s.s_turned, i * 2 + b)
                        act.activation(spT[:, 0:PAGES, :].rearrange("p g h -> p (g h)"), mis[2][:, 0:PAGES * H],
                                       ACT.Copy).then_inc(s.s_pT, 1)
                        act.activation(spT[0:NB, PAGES, :], mis[2][0:NB, PAGES * H:(PAGES + 1) * H],
                                       ACT.Copy).then_inc(s.s_pT, 1)

            sample_step(0, 0, True, False)
            with act.Fori(0, NB // 2 - 1) as i:
                sample_step(i, 1, True, True)
                sample_step(i, 2, True, True)
            sample_step(0, NB - 1, True, True)
            sample_step(0, NB, False, True)

            def exps(h):
                k = h % 2
                act.wait_ge(s.sm_step, 6 * h + 5)
                act.activation(sm[:, k, 0:P], sm[:, k, 0:P], ACT.Exp, scale=ATTN_SCALE,
                               bias=stats[:, 8 * k + 2:8 * k + 3],
                               accum_out=stats[:, 8 * k + 4:8 * k + 5]).then_inc(s.sm_exp, 1)
                act.activation(sm[:, k, P:3 * P], sm[:, k, P:3 * P], ACT.Exp, scale=ATTN_SCALE,
                               bias=stats[:, 8 * k + 3:8 * k + 4],
                               accum_out=stats[:, 8 * k + 5:8 * k + 6]).then_inc(s.sm_exp, 1)

            act.wait_ge(s.ol_ready, NB)
            act.activation(olh[:, :, :, :], olat[:, :, :, :], ACT.Copy).then_inc(s.ol_hi, 1)

            def heads_out(h):
                act.wait_ge(s.o_ps, h + 1)
                act.activation(hh[:, h, :], o_ps[h % 2][:, 0:T], ACT.Copy).then_inc(s.o_hi, 1)
                if h % 2:
                    split(C_UV + 4 + h // 2)

            exps(0)
            for h in range(H):
                if h:
                    heads_out(h - 1)
                if h + 1 < H:
                    exps(h + 1)
                act.wait_ge(s.p_turned, h + 1)
                if h >= 2:
                    act.wait_ge(s.o_ps, h - 1)
                act.activation(pTs[:, h % 2, :], pT_ps[h % 2][:, 0:3 * P], ACT.Copy).then_inc(s.pT_ready, 1)
            heads_out(H - 1)
            with act.Fori(0, 4) as i:
                for c in range(8):
                    split(C_MO + 4 + c, off=i * 8)
            block_norm(2, N_MO, 2 * G_FFN1)
            ramp(N_X3, PT_NORM + 6 * KT, 48, f, C_FFN1)
            root(N_X3, D)
            ffn(1, C_FFN1, H_FFN1)
            block_norm(3, N_F1, 2 * G_END, range(len(mid), len(mid) + 2))
            for n in range(len(mid) + 2, len(plan)):
                rows_out(n)

        @block.vector
        def _(dve):
            def split(c, off=0):
                dve.wait_ge(s.hi_ready, off + (c + 1))
                n = split_width(c)
                dve.tensor_tensor(lo[:, c % SPLIT, :, 0:n], raw[:, c % RAW, :, 0:n],
                                  hi[:, c % SPLIT, :, 0:n].bitcast(F32), ALU.subtract).then_inc(s.lo_ready, 1)

            par = [0]

            def par_op(ins):
                par[0] += 1
                ins.then_inc(s.par_step, 1)
                dve.wait_ge(s.par_step, par[0])

            def row_sums(sq_from):
                dve.tensor_reduce(ssum[:, :], sq_from.rearrange("p j t -> p t j"), AX.X, ALU.add)\
                    .then_inc(s.sum_ready, 1)

            def inverse(n, out):
                dve.wait_ge(s.rms_ready, n + 1)
                dve.reciprocal(out[:, :], rms[:, :]).then_inc(s.rstd_ready, 1)
                dve.wait_ge(s.rstd_ready, n + 1)

            def mean_square(n, sq_from, out):
                dve.wait_ge(s.sq_done, n + 1)
                row_sums(sq_from)
                inverse(n, out)

            def low(dst, dst_hi, base, j, n):
                dve.wait_ge(s.xn_hi, n + j + 1)
                dve.scalar_tensor_tensor(out=dst[:, j, :], in0=x[:, j, :], scalar=PT[:, base + j:base + j + 1],
                                         in1=dst_hi[:, j, :].bitcast(F32), op0=ALU.mult, op1=ALU.subtract)\
                    .then_inc(s.xn_ready, 1)

            def evac(ins):
                ins.then_inc(s.acc_read, 1)

            def low_pair(src, done, tile):
                for m in range(2):
                    dve.wait_ge(s.h_hi, done + (m + 1))
                    dve.tensor_tensor(hl[:, ds(tile + m, 1), :], src[:, m:m + 1, :],
                                      hh[:, ds(tile + m, 1), :].bitcast(F32), ALU.subtract).then_inc(s.h_ready, 1)

            def conv_pair(src, dst, taps, cw, done):
                k_state = taps - 1
                w = NB * k_state
                steps = []
                for k in range(k_state, -1, -1):
                    if k == k_state:
                        steps.append(("now", k, 0))
                        continue
                    steps.append(("past", k, k_state - k))
                    steps.append(("state", k, 0))
                for n, (kind, k, lag) in enumerate(steps):
                    for m in range(2):
                        wk = cw[:, w + k, m:m + 1]
                        if n:
                            dve.wait_ge(s.conv_step, done + (2 * (n - 1) + m + 1))
                        if kind == "now":
                            ins = dve.tensor_scalar(dst(m, 0, T), src[:, m, :], wk, cw[:, w + taps, m:m + 1],
                                                    ALU.mult, ALU.add)
                        elif kind == "past":
                            ins = dve.scalar_tensor_tensor(out=dst(m, lag, S), in0=src[:, m, 0:S - lag], scalar=wk,
                                                           in1=dst(m, lag, S), op0=ALU.mult, op1=ALU.add)
                        else:
                            ins = dve.scalar_tensor_tensor(out=dst(m, S, T), in0=cw[:, k:w:k_state, m], scalar=wk,
                                                           in1=dst(m, S, T), op0=ALU.mult, op1=ALU.add)
                        ins.then_inc(s.conv_step, 1)

            dve.memset(eps[:, :], EPS).then_inc(s.ones_set, 1)
            dve.memset(ones[:, :], 1.0).then_inc(s.ones_set, 1)
            for j in range(KT):
                dve.wait_ge(s.turned, 6 + j + 1)
                dve.tensor_copy(x[:, j, :], mis[(6 + j) % 4][:, 0:T]).then_inc(s.x_tile, 1)
            for c in range(4):
                split(c)

            def ramp_low(n, base, j, xn0, c0):
                low(xnl, xnh, base, j, xn0)
                if j == 11:
                    split(c0 + 4)
                if j == 15:
                    split(c0 + 5)
                if j == KT - 1:
                    split(c0 + 6)
                    dve.wait_ge(s.sq_done, n + 1)
                    row_sums((sq_h if n == N_X0 else f)[:, :, :])
                    split(c0 + 7)

            for j in range(KT):
                ramp_low(N_X0, PT_NORM, j, XN_0, C_RGX)
            inverse(N_X0, rx)

            def conv_pairs(i, leads=(0, 1)):
                for a in range(2):
                    if a in leads:
                        for c in range(4):
                            split(C_RGX + 4 + 4 * a + c, off=i * 8)
                    dve.wait_ge(s.chunk_used, i * 8 + (C_RGX + 4 * a + 4))
                    for m in range(2):
                        evac(dve.tensor_tensor(gs[:, m, :], acc[2 * a + m][:, 0:T], rx[:, :], ALU.mult))
                    dve.wait_ge(s.cw_ready, i * 2 + (a + 1))
                    dve.wait_ge(s.acc_read, i * 4 + (2 * a + 2))

                    def f_tile(m, u, v, i=i, a=a):
                        return f[:, ds(i * 4 + (2 * a + m), 1), u:v].rearrange("p a t -> p (a t)")

                    conv_pair(gs, f_tile, 4, cwr, i * 28 + 14 * a)
                    dve.wait_ge(s.tail_saved, i * 2 + (a + 1))

            conv_pairs(0, leads=(1,))
            lam = PT[:, PT_GATE + 2 * KT:PT_GATE + 3 * KT]
            dve.wait_ge(s.pt_ready, 6)
            dve.wait_ge(s.par_step, 2)
            par[0] = 2
            par_op(dve.tensor_scalar(soft[:, 2, :], soft[:, 1, :], 2.0, None, ALU.add))
            par_op(dve.reciprocal(soft[:, 2, :], soft[:, 2, :]))
            par_op(dve.tensor_tensor(soft[:, 3, :], soft[:, 1, :], soft[:, 2, :], ALU.mult))
            par_op(dve.tensor_tensor(soft[:, 2, :], soft[:, 3, :], soft[:, 3, :], ALU.mult))
            par_op(dve.tensor_scalar(soft[:, 1, :], soft[:, 2, :], 1.0 / 17, None, ALU.mult))
            for k in (15, 13, 11, 9, 7, 5, 3):
                par_op(dve.scalar_tensor_tensor(out=soft[:, 1, :], in0=soft[:, 1, :], scalar=1.0 / k,
                                                in1=soft[:, 2, :], op0=ALU.add, op1=ALU.mult))
            par_op(dve.scalar_tensor_tensor(out=soft[:, 1, :], in0=soft[:, 1, :], scalar=1.0,
                                            in1=soft[:, 3, :], op0=ALU.add, op1=ALU.mult))
            par_op(dve.tensor_scalar(soft[:, 0, :], lam, -1.0, 0.0, ALU.mult, ALU.max))
            par_op(dve.scalar_tensor_tensor(out=soft[:, 1, :], in0=soft[:, 1, :], scalar=2.0,
                                            in1=soft[:, 0, :], op0=ALU.mult, op1=ALU.add))
            par_op(dve.tensor_scalar(lam, soft[:, 1, :], RG_C / 4, None, ALU.mult))
            par_op(dve.tensor_scalar(PT[:, PT_GATE:PT_GATE + 2 * KT], PT[:, PT_GATE:PT_GATE + 2 * KT], 0.5, None,
                                     ALU.mult))
            assert par[0] == PAR_STEPS
            with dve.Fori(1, 4) as i:
                conv_pairs(i)

            def recurrence(i, a):
                tile = i * 4 + 2 * a
                step0 = i * 16 + 8 * a

                def step(ins):
                    ins.then_inc(s.gate_step, 1)

                dve.wait_ge(s.gate_th, i * 6 + (3 * a + 2))
                step(dve.tensor_scalar(r1[:, :, :], ta[:, :, :], 1.0, None, ALU.add))
                dve.wait_ge(s.gate_step, step0 + 1)
                step(dve.reciprocal(r1[:, :, :], r1[:, :, :]))
                step(dve.scalar_tensor_tensor(out=ti[:, :, :], in0=ti[:, :, :], scalar=1.0,
                                              in1=f[:, ds(tile, 2), :], op0=ALU.add, op1=ALU.mult))
                dve.wait_ge(s.gate_step, step0 + 3)
                step(dve.tensor_tensor(ti[:, :, :], ti[:, :, :], r1[:, :, :], ALU.mult))
                dve.wait_ge(s.gate_step, step0 + 4)
                dve.wait_ge(s.gate_th, i * 6 + (3 * a + 3))
                step(dve.tensor_tensor(ti[:, :, :], ti[:, :, :], sq[:, :, :], ALU.mult))
                dve.wait_ge(s.gate_step, step0 + 5)
                dve.wait_ge(s.decay, i * 6 + (3 * a + 3))
                for m in range(2):
                    step(dve.tensor_tensor_scan(
                        f[:, ds(tile + m, 1), 0:S].rearrange("p a t -> p (a t)"), aa[:, m, 0:S],
                        ti[:, m, 0:S], 0.0, ALU.mult, ALU.add))
                step(dve.tensor_tensor(f[:, ds(tile, 2), S:T], aa[:, :, S:T], ti[:, :, S:T], ALU.add))

            def gelu_pair(i, a, following=True):
                tile = i * 4 + 2 * a
                if following:
                    recurrence(i, a + 1)
                for c in range(4):
                    split(C_RGY + 4 + 4 * a + c, off=i * 8)
                dve.wait_ge(s.chunk_used, i * 8 + (C_RGY + 4 * a + 4))
                for m in range(2):
                    evac(dve.tensor_tensor(gs[:, m, :], acc[2 * a + m][:, 0:T], rx[:, :], ALU.mult))
                for m in range(2):
                    dve.wait_ge(s.gelu_done, tile + (m + 1))
                    dve.tensor_tensor(ge[:, m:m + 1, :], ge[:, m:m + 1, :], f[:, ds(tile + m, 1), :], ALU.mult)\
                        .then_inc(s.h_full, 1)
                low_pair(ge, tile, tile)

            recurrence(0, 0)
            with dve.Fori(0, 3) as i:
                for a in range(2):
                    gelu_pair(i, a)
            gelu_pair(3, 0)
            gelu_pair(3, 1, following=False)
            dve.wait_ge(s.ht_saved, 8)
            def project(c0, g0):
                with dve.Fori(0, 4) as i:
                    for a in range(2):
                        for c in range(4):
                            split(c0 + 4 + 4 * a + c, off=i * 8)
                        dve.wait_ge(s.chunk_used, i * 8 + (c0 + 4 * a + 4))
                        for m in range(2):
                            evac(dve.tensor_copy(f[:, ds(i * 4 + (2 * a + m), 1), :].rearrange("p a t -> p (a t)"),
                                                 acc[(2 * (g0 + a) + m) % 4][:, 0:T]))

            def block_norm(b, base, n_f, ready):
                done = 2 * b
                dve.wait_ge(s.sq_step, SQ_STEPS * (b + 1))
                dve.tensor_tensor(ssum[:, :], sq_sum[:, 0, :], sq_sum[:, 1, :], ALU.add).then_inc(s.sum_step, 1)
                dve.wait_ge(s.sum_step, done + 1)
                dve.wait_ge(s.sq_done, n_f + 1)
                dve.tensor_tensor(ssum[:, :], ssum[:, :], sq_last[:, 0, :], ALU.add).then_inc(s.sum_step, 1)
                dve.wait_ge(s.sum_step, done + 2)
                dve.tensor_tensor(ssum[:, :], ssum[:, :], sq_last[:, 1, :], ALU.add).then_inc(s.sum_ready, 1)
                inverse(n_f, rf)
                for j in range(KT):
                    dve.scalar_tensor_tensor(out=f[:, j, :], in0=f[:, j, :], scalar=PT[:, base + j:base + j + 1],
                                             in1=rf[:, :], op0=ALU.mult, op1=ALU.mult).then_inc(s.fnorm, 1)
                    if ready and j >= 3:
                        ready(j - 3)
                if ready:
                    for j in range(KT - 3, KT):
                        ready(j)

            def section(l, c0, g0, h0, sec):
                acc_g, acc_u = 2 * (g0 % 2), 2 * ((g0 + 1) % 2)

                def pair(i, lead=True):
                    off = i * 8
                    if lead:
                        for c in range(4):
                            split(c0 + 4 + c, off=off)
                    dve.wait_ge(s.chunk_used, off + (c0 + 4))
                    dve.wait_ge(s.tail_saved, i + (8 * sec + (8, 32)[l]))
                    for m in range(2):
                        evac(dve.tensor_tensor(gs[:, m, :], acc[acc_g + m][:, 0:T], rx[:, :], ALU.mult))
                    dve.wait_ge(s.cw_ready, i + (8 * sec + (9, 33)[l]))
                    dve.wait_ge(s.acc_read, i * 4 + (2 * g0 + 2))
                    conv_pair(gs, lambda m, u, v: cv[:, m, u:v], 3, cwf, i * 10 + (80 * sec + (CS_FFN0, CS_FFN1)[l]))
                    for c in range(4):
                        split(c0 + 8 + c, off=off)
                    dve.wait_ge(s.chunk_used, off + (c0 + 8))
                    for m in range(2):
                        evac(dve.tensor_tensor(us[:, m, :], acc[acc_u + m][:, 0:T], rx[:, :], ALU.mult))
                    for m in range(2):
                        dve.wait_ge(s.gelu_done, i * 2 + (16 * sec + h0 + m + 1))
                        dve.wait_ge(s.acc_read, i * 4 + (2 * g0 + 3 + m))
                        dve.tensor_tensor(us[:, m, :], us[:, m, :], ge[:, m, :], ALU.mult).then_inc(s.h_full, 1)
                    low_pair(us, i * 2 + (16 * sec + h0), i * 2)

                if sec == 0:
                    pair(0, lead=False)
                with dve.Fori(1 if sec == 0 else 0, 8) as i:
                    pair(i)

                def down(i, leads):
                    for a in range(2):
                        if a in leads:
                            for c in range(4):
                                split(c0 + 68 + 4 * a + c, off=i * 8)
                        dve.wait_ge(s.chunk_used, i * 8 + (c0 + 64 + 4 * a + 4))
                        for m in range(2):
                            ft = f[:, ds(i * 4 + (2 * a + m), 1), :].rearrange("p a t -> p (a t)")
                            ps = acc[(2 * (g0 + a) + m) % 4][:, 0:T]
                            if sec == 0:
                                evac(dve.tensor_copy(ft, ps))
                            else:
                                evac(dve.tensor_tensor(ft, ps, ft, ALU.add))

                last = sec == SECTIONS - 1 and l == 1
                with dve.Fori(0, 3 if last else 4) as i:
                    down(i, (0, 1))
                if last:
                    down(3, (0,))

            def ffn(l, c0, g0, h0):
                for sec in range(SECTIONS):
                    section(l, c0 + 96 * sec, g0 + 24 * sec, h0, sec)

            project(C_RGO, G_RGO)
            dve.wait_ge(s.acc_read, 2 * G_FFN0)
            block_norm(0, PT_NORM + KT, N_RGO,
                       lambda j: ramp_low(N_X1, PT_NORM + 2 * KT, j, XN_1, C_FFN0))
            inverse(N_X1, rx)
            ffn(0, C_FFN0, G_FFN0, H_FFN0)
            dve.wait_ge(s.acc_read, 2 * G_DKV)
            block_norm(1, PT_NORM + 3 * KT, N_F0,
                       lambda j: ramp_low(N_X2, PT_KVIN, j, XN_KV, C_DKV))
            for j in range(KT):
                low(hl, hh, PT_NORM + 4 * KT, j, XN_Q)
            inverse(N_X2, rx)

            def copies(g, dst, c_last, scale=True):
                dve.wait_ge(s.chunk_used, c_last + 1)
                for m in range(2):
                    src = acc[2 * (g % 2) + m][:, 0:T]
                    if scale:
                        evac(dve.tensor_tensor(dst(m), src, rx[:, :], ALU.mult))
                    else:
                        evac(dve.tensor_copy(dst(m), src))

            for a in range(2):
                for c in range(4 if a else 0):
                    split(C_DKV + 8 + c)
                copies(G_DKV + a, lambda m: pre[:, 2 * a + m, :], C_DKV + 4 * a + 3)
            for c in range(4):
                split(C_DKV + 12 + c)
            dve.wait_ge(s.chunk_used, C_DKV + 12)
            g = G_DKV + 2
            dve.tensor_tensor(prk[:, :], acc[2 * (g % 2)][:, 0:T], rx[:, :], ALU.mult).then_inc(s.acc_read, 2)
            dve.wait_ge(s.sq_done, N_C + 1)
            row_sums(sqs[:, :, :])
            for a in range(2):
                for c in range(4):
                    split(C_DQ + 4 + 4 * a + c)
                if a == 0:
                    inverse(N_C, rf)
                copies(G_DQ + a, lambda m: preq[:, 2 * a + m, :], C_DQ + 4 * a + 3)
            dve.wait_ge(s.tail_saved, 32)
            for k in range(LT):
                dve.scalar_tensor_tensor(out=cT[:, k, :], in0=pre[:, k, :], scalar=PT[:, PT_KVN + k:PT_KVN + k + 1],
                                         in1=rf[:, :], op0=ALU.mult, op1=ALU.mult).then_inc(s.c_step, 1)
            dve.tensor_tensor(rot[:, 0, :], prk[:, :], cos_, ALU.mult).then_inc(s.kr_step, 1)
            dve.wait_ge(s.kr_rot, 1)
            dve.tensor_tensor(krT[:, :], mis[2][:, 0:T], sin_, ALU.mult).then_inc(s.kr_step, 1)
            dve.wait_ge(s.kr_step, 2)
            dve.tensor_tensor(krT[:, :], krT[:, :], rot[:, 0, :], ALU.add).then_inc(s.kr_step, 1)
            dve.wait_ge(s.c_hi, 1)
            dve.tensor_tensor(cTl[:, :, :], cT[:, :, :], cTh[:, :, :].bitcast(F32), ALU.subtract).then_inc(s.c_ready, 1)
            mean_square(N_CQ, sqs[:, :, :], rf)
            for k in range(LT):
                dve.scalar_tensor_tensor(out=preq[:, k, :], in0=preq[:, k, :], scalar=PT[:, PT_QN + k:PT_QN + k + 1],
                                         in1=rf[:, :], op0=ALU.mult, op1=ALU.mult).then_inc(s.c_step, 1)
            dve.wait_ge(s.c_hi, 2)
            dve.tensor_tensor(cql[:, :, :], preq[:, :, :], cqh[:, :, :].bitcast(F32), ALU.subtract)\
                .then_inc(s.c_ready, 1)

            def rope(j):
                dve.wait_ge(s.q_rot, j + 1)
                dve.tensor_tensor(rot[:, j % 2, :], qr[:, j, :], cos_, ALU.mult).then_inc(s.q_step, 1)
                dve.wait_ge(s.q_step, 3 * j + 1)
                dve.tensor_tensor(qr[:, j, :], mis[2 + j % 2][:, 0:T], sin_, ALU.mult).then_inc(s.q_step, 1)
                dve.wait_ge(s.q_step, 3 * j + 2)
                dve.tensor_tensor(qr[:, j, :], qr[:, j, :], rot[:, j % 2, :], ALU.add).then_inc(s.q_step, 1)

            for g4 in range(4):
                for e in range(3):
                    c = C_UQ + 3 * g4 + e
                    split(c + 4)
                    if e < 2:
                        copies(G_UQ + 3 * g4 + e, lambda m: qn[:, 4 * g4 + 2 * e + m, :], c, False)
                    else:
                        copies(G_UQ + 3 * g4 + e, lambda m: qr[:, 2 * g4 + m, :], c, False)
                    if e == 0 and g4:
                        rope(2 * g4 - 2)
                        rope(2 * g4 - 1)
            rope(6)
            rope(7)
            dve.wait_ge(s.qs_hi, 1)
            dve.tensor_tensor(qsl[:, :, :], qn[:, :, S:T], qsh[:, :, :].bitcast(F32), ALU.subtract)\
                .then_inc(s.qs_ready, 1)
            for u in range(8):
                split(C_UK + 4 + u)
                for m in range(2):
                    h = 2 * u + m
                    dve.wait_ge(s.uk_hi, h + 1)
                    dve.tensor_tensor(ukTl[:, h % 4, :], mis[m][:, :], ukTh[:, h % 4, :].bitcast(F32), ALU.subtract)\
                        .then_inc(s.uk_read, 1)
                dve.wait_ge(s.chunk_used, C_UK + u + 1)
                for m in range(2):
                    evac(dve.tensor_copy(kn[:, 2 * u + m, :], acc[2 * ((G_UK + u) % 2) + m][:, 0:S]))

            def sample_step(i, b, pages, post):
                def key(g):
                    if pages:
                        dve.wait_ge(s.pg_turned, i * 16 + (8 * b + g + 1))
                        dve.tensor_copy(krp[:, g % 2, :], acc[2 + g % 2][0:ROPE, 0:P]).then_inc(s.pg_k, 1)

                def after(n):
                    dve.wait_ge(s.s_step, i * 12 + (6 * (b - 1) + n))

                if post:
                    dve.wait_ge(s.s_scored, i * 2 + b)
                    dve.tensor_copy(sp_[:, 0:512], mis[0][0:H, :]).then_inc(s.s_step, 1)
                    dve.tensor_copy(sp_[:, 512:1024], mis[1][0:H, :]).then_inc(s.s_step, 1)
                    own = kc[0:H, ds(i * 2 * NB + (K_OWN + (b - 1) * NB), NB)]
                    dve.tensor_tensor(sp_[:, 1024:KEYS], mis[2][0:H, 0:NB], own, ALU.add).then_inc(s.s_step, 1)
                key(0)
                if post:
                    after(3)
                    dve.tensor_reduce(stats[0:H, 0:1], sp_[:, :], AX.X, ALU.max).then_inc(s.s_step, 1)
                    after(4)
                    dve.tensor_scalar(stats[0:H, 1:2], stats[0:H, 0:1], -ATTN_SCALE, None, ALU.mult)\
                        .then_inc(s.s_step, 1)
                key(1)
                key(2)
                if post:
                    dve.wait_ge(s.s_exp, i * 2 + b)
                    dve.reciprocal(stats[0:H, 3:4], stats[0:H, 2:3]).then_inc(s.s_step, 1)
                key(3)
                key(4)
                if post:
                    dve.wait_ge(s.s_out, i * 2 + b)
                    after(6)
                    dve.tensor_scalar(sout[:, :], mis[3][0:H, :], stats[0:H, 3:4], None, ALU.mult)\
                        .then_inc(s.s_norm, 1)
                key(5)
                key(6)
                if post:
                    dve.wait_ge(s.so_turned, i * 2 + b)
                    dve.tensor_copy(olat[:, :, :, ds(i * 2 + (b - 1), 1)].rearrange("p c h b -> p c (h b)"),
                                    mis[2][:, 256:256 + LT * H].rearrange("p (c h) -> p c h", c=LT))\
                        .then_inc(s.ol_ready, 1)
                key(7)

            sample_step(0, 0, True, False)
            with dve.Fori(0, NB // 2 - 1) as i:
                sample_step(i, 1, True, True)
                sample_step(i, 2, True, True)
            sample_step(0, NB - 1, True, True)
            sample_step(0, NB, False, True)

            def soft_a(h):
                k = h % 2
                sc = mis[k]
                dve.wait_ge(s.scored, h + 1)
                diag = sm[:, k, :].rearrange("p (b q) -> p b q", q=P)[:, 0:3:2, :]
                dps = sc[:, 0:3 * P].rearrange("p (b q) -> p b q", q=P)[:, 0:3:2, :]
                mk = mask.rearrange("p (a q) -> p a q", a=1).to_broadcast([P, 2, P])
                dve.tensor_tensor(diag, dps, mk, ALU.add).then_inc(s.sm_step, 1)
                dve.tensor_copy(sm[:, k, P:2 * P], sc[:, P:2 * P]).then_inc(s.sm_step, 1)
                dve.wait_ge(s.sm_step, 6 * h + 2)
                dve.tensor_reduce(stats[:, 8 * k:8 * k + 1], sm[:, k, 0:P], AX.X, ALU.max).then_inc(s.sm_step, 1)
                dve.tensor_reduce(stats[:, 8 * k + 1:8 * k + 2], sm[:, k, P:3 * P], AX.X, ALU.max)\
                    .then_inc(s.sm_step, 1)
                dve.wait_ge(s.sm_step, 6 * h + 4)
                dve.tensor_scalar(stats[:, 8 * k + 2:8 * k + 4], stats[:, 8 * k:8 * k + 2], -ATTN_SCALE, None,
                                  ALU.mult).then_inc(s.sm_step, 1)

            def values(u):
                dve.wait_ge(s.chunk_used, C_UV + u + 1)
                if u >= 2:
                    dve.wait_ge(s.o_ps, 2 * (u - 1))
                dve.tensor_copy(Vs[:, u % 2, :, :].rearrange("p m n -> p (m n)"), acc[2 * ((G_UV + u) % 2)][:, :])\
                    .then_inc(s.acc_read, 2)

            def heads_out(h):
                dve.wait_ge(s.o_hi, h + 1)
                dve.tensor_tensor(hl[:, h, :], o_ps[h % 2][:, 0:T], hh[:, h, :].bitcast(F32), ALU.subtract)\
                    .then_inc(s.o_ready, 1)
                if h % 2:
                    split(C_UV + 4 + h // 2)

            dve.wait_ge(s.ol_hi, 1)
            dve.tensor_tensor(oll[:, :, :, :], olat[:, :, :, :], olh[:, :, :, :].bitcast(F32), ALU.subtract)\
                .then_inc(s.ol_split, 1)
            soft_a(0)
            values(0)
            for h in range(H):
                k = h % 2
                dve.wait_ge(s.sm_exp, 2 * h + 2)
                dve.reciprocal(stats[:, 8 * k + 6:8 * k + 8], stats[:, 8 * k + 4:8 * k + 6]).then_inc(s.sm_step, 1)
                dve.wait_ge(s.sm_step, 6 * h + 6)
                for q, (u, v) in enumerate(((0, P), (P, 3 * P))):
                    dve.tensor_scalar(sm[:, k, u:v], sm[:, k, u:v], stats[:, 8 * k + 6 + q:8 * k + 7 + q], None,
                                      ALU.mult).then_inc(s.prob, 1)
                if h + 1 < H:
                    soft_a(h + 1)
                if h:
                    heads_out(h - 1)
                if k == 0 and h + 2 < H:
                    values(h // 2 + 1)
            heads_out(H - 1)
            project(C_MO, G_MO)
            dve.wait_ge(s.acc_read, 2 * G_FFN1)
            block_norm(2, PT_NORM + 5 * KT, N_MO,
                       lambda j: ramp_low(N_X3, PT_NORM + 6 * KT, j, XN_3, C_FFN1))
            inverse(N_X3, rx)
            ffn(1, C_FFN1, G_FFN1, H_FFN1)
            dve.wait_ge(s.acc_read, 2 * G_END)
            block_norm(3, PT_NORM + 7 * KT, N_F1, None)

        @block.tensor
        def _(pe):
            def mm3(out, wh, wl, xh, xl, start, stop):
                pe.matmul(out, wh, xh, start=start, stop=False)
                pe.matmul(out, wh, xl, start=False, stop=False)
                return pe.matmul(out, wl, xh, start=False, stop=stop)

            def group(c, n, g, xh, xl, ready, g_off=0, c_off=0, tiles=2, between=None):
                if isinstance(g_off, int):
                    if g + g_off >= 2:
                        pe.wait_ge(s.acc_read, 2 * (g + g_off - 1))
                else:
                    pe.wait_ge(s.acc_read, g_off * 2 + 2 * (g - 1))
                for q in range(n):
                    if between and q == 2:
                        between()
                    ready(q)
                    pe.wait_ge(s.lo_ready, c_off + (c + q + 1))
                    slot = (c + q) % SPLIT
                    for m in range(tiles):
                        for k in range(4):
                            kk = 4 * q + k
                            w = (slice(None), slot, k, slice(m * P, m * P + P))
                            last = mm3(acc[2 * (g % 2) + m][:, 0:T], hi[w], lo[w], xh[:, kk, :], xl[:, kk, :],
                                       start=kk == 0, stop=kk == 4 * n - 1)
                    last.then_inc(s.chunk_used, 1)

            def stream(c0, g0, xh, xl, ready, first=0):
                if first:
                    for a in range(2):
                        group(c0 + 4 * a, 4, g0 + a, xh, xl, ready)
                with pe.Fori(first, 4) as i:
                    for a in range(2):
                        group(c0 + 4 * a, 4, g0 + a, xh, xl, ready, g_off=i * 2, c_off=i * 8)

            def xn(base):
                return lambda q: pe.wait_ge(s.xn_ready, base + 4 * (q + 1))

            def row_sum(n):
                pe.wait_ge(s.sum_ready, n + 1)
                pe.matmul(mis[3][:, 0:T], ones[:, :], ssum[:, :], start=True, stop=True).then_inc(s.stat_ready, 1)

            pe.wait_ge(s.const_in, 16)
            pe.wait_ge(s.rows_in[0], 16 * (len(row_pieces) - len(row_pieces[0::4])))
            pe.wait_ge(s.rows_in[1], 16 * len(row_pieces[0::4]))
            for n in range(6):
                if n >= 4:
                    pe.wait_ge(s.pt_ready, n - 3)
                for k in range(4 * n, min(4 * n + 4, PT_TILES)):
                    m = min(P, PT_END - P * k)
                    last = pe.transpose(mis[n % 4][:, P * (k % 4):P * (k % 4) + m], ptrows[0:m, k, :],
                                        ident[0:m, 0:m])
                last.then_inc(s.turned, 1)
            pe.wait_ge(s.x_in, 32)
            for j in range(KT):
                n = 6 + j
                if n < 10:
                    pe.wait_ge(s.pt_ready, n - 3)
                else:
                    pe.wait_ge(s.x_tile, n - 9)
                bank = mis[n % 4]
                for t in range(2):
                    pe.transpose(bank[:, P * t:P * t + P], xrows[:, t, P * j:P * j + P], ident)
                pe.transpose(bank[:, S:T], xsrows[:, P * j:P * j + P], ident[0:NB, 0:NB]).then_inc(s.turned, 1)
            pe.wait_ge(s.ones_set, 2)
            for a in range(2):
                group(4 * a, 4, a, xnh, xnl, xn(XN_0), between=(lambda: row_sum(N_X0)) if a else None)
            with pe.Fori(1, 4) as i:
                for a in range(2):
                    group(4 * a, 4, a, xnh, xnl, xn(XN_0), g_off=i * 2, c_off=i * 8)
            def gates(i, b):
                a = b % 2
                pe.wait_ge(s.gw_loaded[a], i * 32 + 32 * (b // 2 + 1))
                if b:
                    pe.wait_ge(s.gate_tanh, i * 8 + 4 * b)
                for e in range(2):
                    for m in range(2):
                        for k in range(2):
                            last = pe.matmul(mis[2 * e + m][:, 0:T], gw[:, a, 2 * e + k, m * P:m * P + P],
                                             f[:, ds(i * 4 + (2 * b + k), 1), :].rearrange("p a t -> p (a t)"),
                                             start=k == 0, stop=k == 1)
                last.then_inc(s.gates, 1)

            def gelu_pair(i, a, following=True):
                if following:
                    gates(i, a + 1)
                group(C_RGY + 4 * a, 4, G_RGY + a, xnh, xnl, xn(XN_0), g_off=i * 2, c_off=i * 8)

            pe.wait_ge(s.conv_step, 14 * 8)
            gates(0, 0)
            with pe.Fori(0, 3) as i:
                for a in range(2):
                    gelu_pair(i, a)
            gelu_pair(3, 0)
            gelu_pair(3, 1, following=False)
            stream(C_RGO, G_RGO, hh, hl, lambda q: pe.wait_ge(s.h_ready, 4 * (q + 1)))

            def ffn(c00, g00, h0, xbase, n_x):
                for sec in range(SECTIONS):
                    c0, g0 = c00 + 96 * sec, g00 + 24 * sec

                    def pair(i, between=None):
                        group(c0, 4, g0, xnh, xnl, xn(xbase), g_off=i * 2, c_off=i * 8)
                        group(c0 + 4, 4, g0 + 1, xnh, xnl, xn(xbase), g_off=i * 2, c_off=i * 8, between=between)

                    if sec == 0:
                        pair(0, lambda: row_sum(n_x))
                    with pe.Fori(1 if sec == 0 else 0, 8) as i:
                        pair(i)
                    stream(c0 + 64, g0 + 16, hh, hl, lambda q: pe.wait_ge(s.h_ready, 16 * sec + h0 + 4 * (q + 1)))

            row_sum(N_RGO)
            ffn(C_FFN0, G_FFN0, H_FFN0, XN_1, N_X1)
            row_sum(N_F0)
            group(C_DKV, 4, G_DKV, xnh, xnl, xn(XN_KV))
            group(C_DKV + 4, 4, G_DKV + 1, xnh, xnl, xn(XN_KV), between=lambda: row_sum(N_X2))
            group(C_DKV + 8, 4, G_DKV + 2, xnh, xnl, xn(XN_KV), tiles=1)
            for a in range(2):
                group(C_DQ + 4 * a, 4, G_DQ + a, hh, hl, xn(XN_Q), between=None if a else lambda: row_sum(N_C))
            pe.wait_ge(s.acc_read, 2 * G_DQ)
            pe.matmul(mis[2][:, 0:T], swap, prk[:, :], start=True, stop=True).then_inc(s.kr_rot, 1)
            def turn_out(n):
                if n >= 2:
                    pe.wait_ge(s.out_rows, n - 1 if n < len(mid) + 3 else n - 2)
                tiles, m, _ = plan[n]
                col = 0
                for t in tiles:
                    w = t.shape[0]
                    last = pe.transpose(row_bank(n)[0:m, col:col + w], t, ident[0:w, 0:w])
                    col += w
                last.then_inc(s.out_turned, 1)

            pe.wait_ge(s.tail_saved, 32)
            pe.wait_ge(s.ht_saved, 8)
            for n in range(MID_BEFORE):
                turn_out(n)
            row_sum(N_CQ)
            for n in range(MID_BEFORE, MID_STALL):
                turn_out(n)

            def rotate(j):
                pe.wait_ge(s.acc_read, 2 * (G_UQ + 3 * (j // 2) + 3))
                if j >= 2:
                    pe.wait_ge(s.q_step, 3 * (j - 1))
                else:
                    pe.wait_ge(s.kr_step, 3)
                pe.matmul(mis[2 + j % 2][:, 0:T], swap, qr[:, j, :], start=True, stop=True).then_inc(s.q_rot, 1)

            for g4 in range(4):
                for e in range(3):
                    g = G_UQ + 3 * g4 + e
                    group(C_UQ + 3 * g4 + e, 1, g, cqh, cql, lambda q: pe.wait_ge(s.c_ready, 2))
                    if e == 0 and g4:
                        rotate(2 * g4 - 2)
                        rotate(2 * g4 - 1)
                    for n in mid_with(3 * g4 + e):
                        turn_out(n)
            pe.wait_ge(s.acc_read, 2 * G_UK)
            rotate(6)
            rotate(7)
            pe.wait_ge(s.q_step, 24)

            pe.wait_ge(s.out_rows, len(mid))
            for k in range(LT):
                last = pe.transpose(mis[0][0:NB, P * k:P * k + P], cT[:, k, S:T], ident)
            last.then_inc(s.cn_turned, 1)
            pe.matmul(mis[1][0:ROPE, 0:NB * H // 2], ident[:, ROPE:P], qr[:, :, S:T].rearrange("p g b -> p g b"),
                      start=True, stop=True).then_inc(s.sh_done, 1)
            pe.wait_ge(s.cn_ready, 1)
            pe.wait_ge(s.sh_ready, 1)
            pe.wait_ge(s.out_rows, len(mid))
            def latent_queries(u):
                for m in range(2):
                    h = 2 * u + m
                    pe.wait_ge(s.uk_read, h + 1)
                    if u >= 1:
                        pe.wait_ge(s.ql_ready, h - 1)
                    for k in range(4):
                        w = (slice(None), h % 4, slice(P * k, P * k + P))
                        last = mm3(mis[2 + m][:, NB * k:NB * k + NB], ukTh[w], ukTl[w], qsh[:, h, :], qsl[:, h, :],
                                   start=True, stop=True)
                    last.then_inc(s.ql_done, 1)

            pe.wait_ge(s.qs_ready, 1)
            for u in range(8):
                c = C_UK + u
                pe.wait_ge(s.lo_ready, c + 1)
                for m in range(2):
                    if u >= 1:
                        pe.wait_ge(s.uk_read, 2 * u - 1 + m)
                    for k in range(4):
                        last = pe.transpose(mis[m][:, P * k:P * k + P], raw[:, c % RAW, k, P * m:P * m + P], ident)
                    last.then_inc(s.uk_turned, 1)
                pe.wait_ge(s.acc_read, 2 * (G_UK + u - 1))
                for m in range(2):
                    for k in range(4):
                        w = (slice(None), c % SPLIT, k, slice(m * P, m * P + P))
                        last = mm3(acc[2 * ((G_UK + u) % 2) + m][:, 0:S], hi[w], lo[w], cTh[:, k, 0:S],
                                   cTl[:, k, 0:S], start=k == 0, stop=k == 3)
                last.then_inc(s.chunk_used, 1)
                if u:
                    latent_queries(u - 1)
            latent_queries(7)

            pe.wait_ge(s.acc_read, 2 * G_UV)
            pe.wait_ge(s.ql_ready, H)
            def sample_step(i, b, pages, post):
                a, k2 = b % 2, (b - 1) % 2

                def turn_page(g):
                    if g % 4 == 0:
                        pe.wait_ge(s.page_in[2 * a + g // 4], i * 128 + 128 * (b // 2 + 1))
                    for k in range(LT):
                        pe.transpose(acc[g % 2][:, P * k:P * k + P],
                                     cpage[:, 2 * a + g // 4, g % 4, P * k:P * k + P], ident)
                    pe.transpose(acc[2 + g % 2][0:ROPE, 0:P], kpage[:, 2 * a + g // 4, g % 4, :], ident)\
                        .then_inc(s.pg_turned, 1)

                def score_page(g):
                    pe.wait_ge(s.pg_c, i * 16 + (8 * b + g + 1))
                    pe.wait_ge(s.pg_k, i * 16 + (8 * b + g + 1))
                    out = mis[g // 4][0:H, P * (g % 4):P * (g % 4) + P]
                    for k in range(LT):
                        pe.matmul(out, qb[:, k, :], ctp[:, g % 2, k, :], start=k == 0, stop=False)
                    return pe.matmul(out, qrb[:, :], krp[:, g % 2, :], start=False, stop=True)

                if pages:
                    turn_page(0)
                    pe.wait_ge(s.qb_ready, i * 4 + (2 * b + 2))
                for g in range(PAGES):
                    if pages:
                        if g + 1 < PAGES:
                            turn_page(g + 1)
                        score_page(g)
                    if post and g == 2:
                        pe.wait_ge(s.s_exp, i * 2 + b)
                        pe.matmul(mis[2][:, 0:H], sp_[:, 0:P], ident[0:H, 0:H], start=True, stop=True)
                        for p in range(1, PAGES):
                            pe.transpose(mis[2][:, H * p:H * p + H], sp_[:, P * p:P * p + P], ident[0:H, 0:H])
                        pe.transpose(mis[2][0:NB, PAGES * H:PAGES * H + H], sp_[:, PAGES * P:KEYS],
                                     ident[0:H, 0:H]).then_inc(s.s_turned, 1)
                    if post and g == 3:
                        pe.wait_ge(s.s_pT, i * 4 + 2 * b)
                        for p in range(PAGES):
                            pe.matmul(mis[3][0:H, :], spT[:, p, :], cpage[:, 2 * k2 + p // 4, p % 4, :],
                                      start=p == 0, stop=False)
                        pe.matmul(mis[3][0:H, :], spT[0:NB, PAGES, :], cnew[:, :], start=False, stop=True)\
                            .then_inc(s.s_out, 1)
                    if post and g == 5:
                        pe.wait_ge(s.s_norm, i * 2 + b)
                        pe.matmul(mis[2][:, 256:256 + H], sout[:, 0:P], ident[0:H, 0:H], start=True, stop=True)
                        for k in range(1, LT):
                            last = pe.transpose(mis[2][:, 256 + H * k:256 + H * k + H], sout[:, P * k:P * k + P],
                                                ident[0:H, 0:H])
                        last.then_inc(s.so_turned, 1)
                if pages:
                    new = mis[2][0:H, 0:NB]
                    if post:
                        pe.wait_ge(s.ol_ready, i * 2 + b)
                    for k in range(LT):
                        pe.matmul(new, qb[:, k, :], cT[:, k, S:T], start=k == 0, stop=False)
                    pe.matmul(new, qrb[:, :], krT[0:ROPE, S:T], start=False, stop=True).then_inc(s.s_scored, 1)

            sample_step(0, 0, True, False)
            with pe.Fori(0, NB // 2 - 1) as i:
                sample_step(i, 1, True, True)
                sample_step(i, 2, True, True)
            sample_step(0, NB - 1, True, True)

            def value_pair(u):
                c, g = C_UV + u, G_UV + u
                pe.wait_ge(s.lo_ready, c + 1)
                pe.wait_ge(s.acc_read, 2 * (g - 1))
                for m in range(2):
                    for k in range(4):
                        keys = slice(m * P, m * P + P)
                        ah, al = cTh[:, k, keys], cTl[:, k, keys]
                        out = acc[2 * (g % 2)][:, 256 * m:256 * m + 256]
                        last = mm3(out, ah, al, hi[:, c % SPLIT, k, :], lo[:, c % SPLIT, k, :], k == 0, k == 3)
                last.then_inc(s.chunk_used, 1)

            value_pair(0)
            sample_step(0, NB, False, True)
            pe.wait_ge(s.ol_ready, NB)

            def scores(h):
                out = mis[h % 2]
                half = slice(ROPE * (h % 2), ROPE * (h % 2) + ROPE)
                for q in range(2):
                    o = out[:, P * q:P * q + P * (q + 1)]
                    pe.matmul(o, qn[:, h, P * q:P * q + P], kn[:, h, 0:P * (q + 1)], start=True, stop=False)
                    last = pe.matmul(o, qr[half, h // 2, P * q:P * q + P], krT[half, 0:P * (q + 1)],
                                     start=False, stop=True)
                last.then_inc(s.scored, 1)

            def output(h):
                u = h // 2
                pe.wait_ge(s.pT_ready, h + 1)
                pe.wait_ge(s.acc_read, 2 * (G_UV + u + 1))
                if h >= 2:
                    pe.wait_ge(s.o_ready, h - 1)
                out = o_ps[h % 2]
                v = slice(P * (h % 2), P * (h % 2) + P)
                pe.matmul(out[:, 0:S], Vs[:, u % 2, 0, v], pTs[:, h % 2, 0:S], start=True, stop=False,
                          skip_group_check=True)
                pe.matmul(out[:, P:S], Vs[:, u % 2, 1, v], pTs[:, h % 2, S:S + P], start=False, stop=False,
                          skip_group_check=True)
                for k in range(4):
                    w = (slice(None), (C_UV + u) % SPLIT, k, v)
                    for n, (a, b) in enumerate(((hi, olh), (hi, oll), (lo, olh))):
                        last = pe.matmul(out[:, S:T], a[w], b[:, k, h, :], start=False, stop=k == 3 and n == 2,
                                         skip_group_check=True)
                last.then_inc(s.o_ps, 1)

            scores(0)
            pe.wait_ge(s.ol_split, 1)
            for h in range(H):
                if h + 1 < H:
                    scores(h + 1)
                if h:
                    output(h - 1)
                if h % 2 == 0 and h + 2 < H:
                    value_pair(h // 2 + 1)
                pe.wait_ge(s.prob, 2 * h + 2)
                for b in range(3):
                    last = pe.transpose(pT_ps[h % 2][:, P * b:P * b + P], sm[:, h % 2, P * b:P * b + P], ident)
                last.then_inc(s.p_turned, 1)
            output(H - 1)
            pe.wait_ge(s.o_ready, H - 1)
            stream(C_MO, G_MO, hh, hl, lambda q: pe.wait_ge(s.o_ready, 4 * (q + 1)))
            row_sum(N_MO)
            ffn(C_FFN1, G_FFN1, H_FFN1, XN_3, N_X3)
            pe.wait_ge(s.tail_saved, 56)
            for n in range(len(mid), len(mid) + 2):
                turn_out(n)
            row_sum(N_F1)
            for n in range(len(mid) + 2, len(plan)):
                if n == len(mid) + FT // 4:
                    pe.wait_ge(s.x_tile, 16 * 5)
                turn_out(n)


_INS = ["x_prompt", "x_sample", "state_rglru_h", "state_rglru_conv", "state_ffn_conv", "cache_kv_latent",
        "cache_k_rope", "page_table", "norm_g", "w_rg_in", "conv_rg_w", "conv_rg_b", "w_rg_a", "b_rg_a",
        "w_rg_i", "b_rg_i", "rg_lambda", "w_rg_o", "kv_in_g", "w_dkv", "kv_norm_g", "w_uk", "w_uv", "w_dq",
        "q_norm_g", "w_uq", "w_mla_o", "w_ffn_g", "w_ffn_u", "ffn_conv_w", "ffn_conv_b", "w_ffn_d"]
_OUTS = {"y_p": (1, S, D), "y_s": (NB, 1, D), "p_h": (1, 1, D), "s_h": (1, NB, D), "p_rgc": (1, 1, 3, D),
         "s_rgc": (1, NB, 3, D), "p_ffc": (2, 1, 2, FF), "s_ffc": (2, NB, 2, FF), "p_kv": (1, S, LORA),
         "s_kv": (NB, 1, LORA), "p_kr": (1, S, ROPE), "s_kr": (NB, 1, ROPE)}


def shape_constants():
    import numpy as np

    k = np.zeros((P, K_END), np.float32)
    k[:, K_ID:K_ID + P] = np.eye(P)
    half = ROPE // 2
    inv = np.float32(10000.0) ** (-np.arange(half, dtype=np.float32) * np.float32(2.0) / np.float32(ROPE))
    pos = np.concatenate([np.arange(S), np.full(NB, PAGES * PAGE)]).astype(np.float32)
    ang = (pos[None, :] * inv[np.arange(P) % half][:, None]).astype(np.float32)
    k[:, K_COS:K_COS + T] = np.cos(ang)
    k[:, K_SIN:K_SIN + T] = np.sin(ang)
    k[:, K_MASK:K_MASK + P] = np.where(np.arange(P)[None, :] <= np.arange(P)[:, None], 0.0, -1e30)
    k[:, K_OWN:K_OWN + NB * NB] = np.where(np.eye(NB) > 0, 0.0, -1e30).reshape(1, -1)
    for base in range(0, P, ROPE):
        for m in range(half):
            k[base + m + half, K_SWAP + base + m] = -1.0
            k[base + m, K_SWAP + base + m + half] = 1.0
    return k


def kernel(**inputs):
    import numpy as np
    import concourse.bacc as bacc
    from concourse.bass_utils import run_bass_kernel_spmd

    nc = bacc.Bacc("TRN2", target_bir_lowering=False, num_devices=1)
    arrays, ins, outs = {}, {}, {}
    for name in _INS:
        a = np.ascontiguousarray(inputs[name])
        arrays[f"in_{name}"] = a
        ins[name] = nc.dram_tensor(f"in_{name}", a.shape, mybir.dt.from_np(a.dtype), kind="ExternalInput").ap()
    arrays["in_consts"] = shape_constants()
    ins["consts"] = nc.dram_tensor("in_consts", (P, K_END), F32, kind="ExternalInput").ap()
    for name, shape in _OUTS.items():
        outs[name] = nc.dram_tensor(f"out_{name}", shape, F32, kind="ExternalOutput").ap()
    build(nc, ins, outs)
    r = run_bass_kernel_spmd(nc, [arrays], core_ids=[0])
    return tuple(r.results[0][f"out_{name}"] for name in _OUTS)
```
